# Optimizing a Trainium2 kernel written in Bass

```python
import math
import jax, jax.numpy as jnp
from jax import lax
import numpy as np

D_MODEL = 2048
BATCH = 1
SEQ = 256
DEPTH = 1
DEC_BATCH = 8
DEC_SEQ = 16
PAST_LEN = 256

CHUNK = 64
D_POOL = D_MODEL // 4
POOL_WINDOWS = (2, 4, 8, 16)
N_POOL_GROUPS = len(POOL_WINDOWS)
POOL_GROUP = D_POOL // N_POOL_GROUPS
POOL_HIST = max(POOL_WINDOWS) - 1
D_ATTN = D_MODEL - D_POOL
HEAD_DIM = 64
V_DIM = 2 * HEAD_DIM
N_HEADS = D_ATTN // V_DIM
ROT_DIM = HEAD_DIM // 4
ROPE_THETA = 500000.0
Q_BLOCK = 128
D_IN = D_POOL + 3 * D_ATTN
PEER_HEADS = 8
N_KEYS = 128
N_EXPERTS = N_KEYS * N_KEYS
D_KEY = 256
D_HALF = D_KEY // 2
PEER_TOPK = 16
PEER_BLOCK = 128
EPS = 1e-6

kernel_name = "hybrid_pool_diffattn_peer_stream_step"

def rmsnorm(x, g):
    xf = x.astype(jnp.float32)
    r = lax.rsqrt(jnp.mean(xf * xf, axis=-1, keepdims=True) + EPS)
    return (xf * r * g.astype(jnp.float32)).astype(x.dtype)

def rope_partial(x, pos):
    inv = ROPE_THETA ** (-jnp.arange(0, ROT_DIM, 2, dtype=jnp.float32) / ROT_DIM)
    ang = pos.astype(jnp.float32)[:, None] * inv[None, :]
    cos = jnp.cos(ang)[None, :, None, None, :]
    sin = jnp.sin(ang)[None, :, None, None, :]
    xf = x.astype(jnp.float32)
    half = ROT_DIM // 2
    x1 = xf[..., :half]
    x2 = xf[..., half:ROT_DIM]
    out = jnp.concatenate([x1 * cos - x2 * sin, x2 * cos + x1 * sin, xf[..., ROT_DIM:]], axis=-1)
    return out.astype(x.dtype)

def pool_mixer(u_hist, u_new, pos0, w_pool, pool_scale):
    B, S, _ = u_new.shape
    u = jnp.concatenate([u_hist, u_new], axis=1).astype(jnp.float32)
    cs = jnp.concatenate([jnp.zeros((B, 1, D_POOL), jnp.float32), jnp.cumsum(u, axis=1)], axis=1)
    pos = pos0 + jnp.arange(S)
    end = POOL_HIST + 1
    outs = []
    for g, w in enumerate(POOL_WINDOWS):
        lo, hi = g * POOL_GROUP, (g + 1) * POOL_GROUP
        win_sum = cs[:, end:end + S, lo:hi] - cs[:, end - w:end - w + S, lo:hi]
        cnt = jnp.minimum(pos + 1, w).astype(jnp.float32)[None, :, None]
        d = win_sum / cnt - u_new[..., lo:hi].astype(jnp.float32)
        outs.append(jnp.einsum('bsc,cd->bsd', d, w_pool[g].astype(jnp.float32)))
    out = jnp.concatenate(outs, axis=-1) * pool_scale.astype(jnp.float32)
    new_hist = u[:, -POOL_HIST:].astype(u_new.dtype)
    return out.astype(u_new.dtype), new_hist

def diff_attend(q, q_pos, k, v, k_pos, lam):
    s = jnp.einsum('bqhcd,bkhcd->bhcqk', q, k).astype(jnp.float32) * (HEAD_DIM ** -0.5)
    mask = (k_pos[None, :] // CHUNK) <= (q_pos[:, None] // CHUNK)
    s = jnp.where(mask[None, None, None], s, jnp.finfo(jnp.float32).min)
    p = jax.nn.softmax(s, axis=-1)
    w = p[:, :, 0] - lam * p[:, :, 1]
    return jnp.einsum('bhqk,bkhe->bqhe', w.astype(v.dtype), v)

def peer_block(xb, w_pq, sub_keys, u_tab, v_tab):
    T = xb.shape[0]
    q = (xb @ w_pq).reshape(T, PEER_HEADS, 2, D_HALF)
    s = jnp.einsum('thcd,ckd->thck', q, sub_keys).astype(jnp.float32)
    s1, i1 = lax.top_k(s[:, :, 0], PEER_TOPK)
    s2, i2 = lax.top_k(s[:, :, 1], PEER_TOPK)
    cand = (s1[..., :, None] + s2[..., None, :]).reshape(T, PEER_HEADS, PEER_TOPK * PEER_TOPK)
    cidx = (i1[..., :, None] * N_KEYS + i2[..., None, :]).reshape(T, PEER_HEADS, PEER_TOPK * PEER_TOPK)
    best, sel = lax.top_k(cand, PEER_TOPK)
    eidx = jnp.take_along_axis(cidx, sel, axis=-1)
    g = jax.nn.softmax(best, axis=-1)
    u = jnp.take(u_tab, eidx, axis=0)
    a = jax.nn.gelu(jnp.einsum('thkd,td->thk', u, xb).astype(jnp.float32))
    vv = jnp.take(v_tab, eidx, axis=0)
    return jnp.einsum('thk,thkd->td', (g * a).astype(xb.dtype), vv)

def peer(xn, w_pq, sub_keys, u_tab, v_tab):
    B, S, D = xn.shape
    T = B * S
    n_blk = -(-T // PEER_BLOCK)
    xt = jnp.pad(xn.reshape(T, D), ((0, n_blk * PEER_BLOCK - T), (0, 0)))
    out = lax.map(lambda xb: peer_block(xb, w_pq, sub_keys, u_tab, v_tab),
                  xt.reshape(n_blk, PEER_BLOCK, D))
    return out.reshape(n_blk * PEER_BLOCK, D)[:T].reshape(B, S, D)

def layer(x, k_hist, v_hist, pool_hist, norm1_g, w_in, w_pool, pool_scale, q_norm_g, k_norm_g,
          lambda_q1, lambda_k1, lambda_q2, lambda_k2, subln_g, w_out, norm2_g, w_pq, sub_keys,
          u_tab, v_tab, lam_init):
    B, S, _ = x.shape
    pos0 = k_hist.shape[1]
    pos = pos0 + jnp.arange(S)
    xn = rmsnorm(x, norm1_g)
    proj = xn @ w_in
    u_pool = proj[..., :D_POOL]
    q = proj[..., D_POOL:D_POOL + D_ATTN].reshape(B, S, N_HEADS, 2, HEAD_DIM)
    k = proj[..., D_POOL + D_ATTN:D_POOL + 2 * D_ATTN].reshape(B, S, N_HEADS, 2, HEAD_DIM)
    v = proj[..., D_POOL + 2 * D_ATTN:].reshape(B, S, N_HEADS, V_DIM)
    q = rope_partial(rmsnorm(q, q_norm_g), pos)
    k = rope_partial(rmsnorm(k, k_norm_g), pos)
    pool_out, pool_new = pool_mixer(pool_hist, u_pool, pos0, w_pool, pool_scale)
    k_all = jnp.concatenate([k_hist, k], axis=1)
    v_all = jnp.concatenate([v_hist, v], axis=1)
    k_pos = jnp.arange(pos0 + S)
    lam = (jnp.exp(jnp.sum(lambda_q1.astype(jnp.float32) * lambda_k1.astype(jnp.float32)))
           - jnp.exp(jnp.sum(lambda_q2.astype(jnp.float32) * lambda_k2.astype(jnp.float32)))
           + lam_init)
    if S % Q_BLOCK == 0 and S > Q_BLOCK:
        n_blk = S // Q_BLOCK
        qb = jnp.moveaxis(q.reshape(B, n_blk, Q_BLOCK, N_HEADS, 2, HEAD_DIM), 1, 0)
        pb = pos.reshape(n_blk, Q_BLOCK)
        o = lax.map(lambda a: diff_attend(a[0], a[1], k_all, v_all, k_pos, lam), (qb, pb))
        o = jnp.moveaxis(o, 0, 1).reshape(B, S, N_HEADS, V_DIM)
    else:
        o = diff_attend(q, pos, k_all, v_all, k_pos, lam)
    o = (rmsnorm(o, subln_g).astype(jnp.float32) * (1.0 - lam_init)).astype(x.dtype)
    mix = jnp.concatenate([pool_out, o.reshape(B, S, D_ATTN)], axis=-1) @ w_out
    h = x + mix
    y = h + peer(rmsnorm(h, norm2_g), w_pq, sub_keys, u_tab, v_tab)
    return y, k, v, pool_new

def setup_inputs(seed: int = 0) -> dict:
    key = jax.random.key(seed)
    ks = jax.random.split(key, 24)
    f32 = jnp.float32
    nrm = lambda k, shp: jax.random.normal(k, shp, f32)
    return {
        "x_prompt": nrm(ks[0], (BATCH, SEQ, D_MODEL)),
        "x_sample": nrm(ks[1], (DEC_BATCH, DEC_SEQ, D_MODEL)),
        "cache_k": nrm(ks[2], (DEPTH, DEC_BATCH, PAST_LEN, N_HEADS, 2, HEAD_DIM)),
        "cache_v": nrm(ks[3], (DEPTH, DEC_BATCH, PAST_LEN, N_HEADS, V_DIM)),
        "state_pool": nrm(ks[4], (DEPTH, DEC_BATCH, POOL_HIST, D_POOL)),
        "norm1_g": 1.0 + 0.02 * nrm(ks[5], (DEPTH, D_MODEL)),
        "w_in": nrm(ks[6], (DEPTH, D_MODEL, D_IN)) * D_MODEL ** -0.5,
        "w_pool": nrm(ks[7], (DEPTH, N_POOL_GROUPS, POOL_GROUP, POOL_GROUP)) * POOL_GROUP ** -0.5,
        "pool_scale": 1.0 + 0.02 * nrm(ks[8], (DEPTH, D_POOL)),
        "q_norm_g": 1.0 + 0.02 * nrm(ks[9], (DEPTH, HEAD_DIM)),
        "k_norm_g": 1.0 + 0.02 * nrm(ks[10], (DEPTH, HEAD_DIM)),
        "lambda_q1": 0.1 * nrm(ks[11], (DEPTH, HEAD_DIM)),
        "lambda_k1": 0.1 * nrm(ks[12], (DEPTH, HEAD_DIM)),
        "lambda_q2": 0.1 * nrm(ks[13], (DEPTH, HEAD_DIM)),
        "lambda_k2": 0.1 * nrm(ks[14], (DEPTH, HEAD_DIM)),
        "subln_g": 1.0 + 0.02 * nrm(ks[15], (DEPTH, V_DIM)),
        "w_out": nrm(ks[16], (DEPTH, D_MODEL, D_MODEL)) * D_MODEL ** -0.5,
        "norm2_g": 1.0 + 0.02 * nrm(ks[17], (DEPTH, D_MODEL)),
        "w_pq": nrm(ks[18], (DEPTH, D_MODEL, PEER_HEADS * D_KEY)) * D_MODEL ** -0.5,
        "sub_keys": nrm(ks[19], (DEPTH, 2, N_KEYS, D_HALF)) * D_HALF ** -0.5,
        "u_tab": nrm(ks[20], (DEPTH, N_EXPERTS, D_MODEL)) * D_MODEL ** -0.5,
        "v_tab": nrm(ks[21], (DEPTH, N_EXPERTS, D_MODEL)) * PEER_HEADS ** -0.5,
    }

def reference(x_prompt, x_sample, cache_k, cache_v, state_pool, norm1_g, w_in, w_pool, pool_scale,
              q_norm_g, k_norm_g, lambda_q1, lambda_k1, lambda_q2, lambda_k2, subln_g, w_out,
              norm2_g, w_pq, sub_keys, u_tab, v_tab):
    B = x_prompt.shape[0]
    yp, ys = x_prompt, x_sample
    kp_l, vp_l, pp_l, ks_l, vs_l, ps_l = [], [], [], [], [], []
    for l in range(DEPTH):
        lam_init = 0.8 - 0.6 * math.exp(-0.3 * (l + 1))
        params = (norm1_g[l], w_in[l], w_pool[l], pool_scale[l], q_norm_g[l], k_norm_g[l],
                  lambda_q1[l], lambda_k1[l], lambda_q2[l], lambda_k2[l], subln_g[l], w_out[l],
                  norm2_g[l], w_pq[l], sub_keys[l], u_tab[l], v_tab[l])
        k0 = jnp.zeros((B, 0, N_HEADS, 2, HEAD_DIM), yp.dtype)
        v0 = jnp.zeros((B, 0, N_HEADS, V_DIM), yp.dtype)
        p0 = jnp.zeros((B, POOL_HIST, D_POOL), yp.dtype)
        yp, kp, vp, pp = layer(yp, k0, v0, p0, *params, lam_init)
        ys, ks_, vs_, ps_ = layer(ys, cache_k[l], cache_v[l], state_pool[l], *params, lam_init)
        kp_l.append(kp); vp_l.append(vp); pp_l.append(pp)
        ks_l.append(ks_); vs_l.append(vs_); ps_l.append(ps_)
    return (yp, ys, jnp.stack(kp_l), jnp.stack(vp_l), jnp.stack(pp_l),
            jnp.stack(ks_l), jnp.stack(vs_l), jnp.stack(ps_l))


_drawn_inputs = setup_inputs


def setup_inputs(seed=0):
    import zlib

    import numpy as np

    out = dict(_drawn_inputs(seed))
    spreads = {}
    factors = {'pool_scale': 50.08, 'q_norm_g': 2.983, 'subln_g': 36.058, 'norm2_g': 19.117}
    for name, (base, spread) in spreads.items():
        noise = np.random.default_rng([zlib.crc32(name.encode()), seed]).standard_normal(out[name].shape)
        drawn = base * np.exp(spread * noise) if base else spread * noise
        out[name] = __import__('jax').numpy.asarray(drawn.astype(out[name].dtype))
    for name, factor in factors.items():
        out[name] = (out[name] * factor).astype(out[name].dtype)
    return out
```

```python
import math
from contextlib import ExitStack

import numpy as np

import concourse.bass as bass
from concourse import mybir

P = 128
D = 2048
KC = D // P
SEQ, DEC_B, DEC_S, PAST = 256, 8, 16, 256
NT = (SEQ + DEC_B * DEC_S) // P
T = NT * P
DPOOL, DATT, HEADS, HD, VD = 512, 1536, 12, 64, 128
NG = 3
HG = HEADS // NG
GW = HG * VD
HIST = 15
PH, TOPK, NKEY = 8, 16, 128
EPS = 1e-6
LAM_INIT = 0.8 - 0.6 * math.exp(-0.3)
QS = HD ** -0.5
NEG = -3.0e38
W = 512
KQ = 4
TB = 16
NTB = T // TB
N_WIN, N_WOUT, N_WPQ = 40, 16, 16
BASE_POOL = 36
BASE_WOUT = N_WIN
BASE_WPQ = BASE_WOUT + N_WOUT
BASE_U = BASE_WPQ + N_WPQ
BASE_V = BASE_U + P
N_PARTS = 18
U_ROUTE = NT * N_PARTS
U_DENSE = 4 * (NTB // 2)
U_REST = P - U_ROUTE - U_DENSE

C_ID, C_IOTA, C_ROPE, C_PM, C_SM, C_SEL, C_CV, C_INV = 0, 128, 256, 304, 368, 608, 736, 738
C_END = C_INV + 64 + 6


def constants():
    c = np.zeros((P, C_END), np.float32)
    c[:, C_ID:C_ID + P] = np.eye(P, dtype=np.float32)
    c[:, C_IOTA:C_IOTA + P] = np.arange(P, dtype=np.float32)
    inv = np.float32(500000.0) ** (-np.arange(0, 16, 2, dtype=np.float32) / np.float32(16))
    pos = np.concatenate([np.arange(SEQ), PAST + np.arange(P) % DEC_S]).astype(np.float32)
    ang = (pos[:, None] * inv[None, :].astype(np.float32)).astype(np.float32)
    rope = np.stack([np.cos(ang), np.sin(ang)], 1).astype(np.float32)
    c[:, C_ROPE:C_PM] = rope.reshape(NT, P, 16).transpose(1, 0, 2).reshape(P, 48)
    c[0:64, C_PM:C_SM] = NEG
    c[:, C_SM:C_SEL] = NEG
    c[:, C_SM + 112:C_SM + 128] = 0.0
    for h in range(HG):
        for m in range(2):
            for q in range(DEC_S):
                c[32 * h + 16 * m + q, C_SEL + 32 * h + q] = 1.0
            c[32 * h + 16 * m:32 * h + 16 * m + 16, C_CV + m] = 1.0
    for g in range(4):
        w = 2 ** (g + 1)
        c[:, C_INV + 16 * g:C_INV + 16 * g + 16] = 1.0 / np.minimum(np.arange(16) + 1, w)
    return c


def hybrid_layer(nc, I, O):
    F32, F32R, U32 = mybir.dt.float32, mybir.dt.float32r, mybir.dt.uint32
    ALU, ACT, AX = mybir.AluOpType, mybir.ActivationFunctionType, mybir.AxisListType
    ds = bass.ds
    ctx = ExitStack()
    with ctx:
        ctx.enter_context(nc.allow_non_contiguous_dma(reason="small vectors"))
        KB = 1024
        base = (nc.sbuf_base + 63) // 64 * 64
        arena = ctx.enter_context(nc.sbuf_tensor("arena", [P, 207 * 256], F32, align_bytes=64))

        def at(name, kb, shape, dt=F32):
            return nc.alloc_sbuf_tensor_at(name, shape, dt, offset=base + int(kb * KB))

        xTh = at("xT_hi", 0, [P, KC, T], F32R)
        xTl = at("xT_lo", 24, [P, KC, T], F32R)
        ringH = at("ring_hi", 48, [P, 2, D], F32R)
        ringL = at("ring_lo", 64, [P, 2, D], F32R)
        raw = at("raw", 80, [P, 2, D])
        cst = at("cst", 96, [P, C_END])
        m0 = 96 + (C_END * 4) / KB
        prm = at("prm", m0, [P, 512])
        MX, WK = 101.5, 149.5
        mixTh = at("mixT_hi", MX, [P, KC, T], F32R)
        mixTl = at("mixT_lo", MX + 24, [P, KC, T], F32R)
        gqk = prm[:, 0:128].rearrange("p (c d) -> p c d", c=2)
        pscale = prm[:, 128:132]
        subg = prm[:, 132:133]
        lamv = prm[:, 133:134]
        cvec = prm[:, 134:135]
        cvt = prm[:, 135:136]
        lame = prm[:, 136:138]
        ssx = prm[:, 140:143]
        rtx = prm[:, 144:147]
        rrx = prm[:, 148:151]
        ss48 = prm[:, 152:200]
        rt48 = prm[:, 200:248]
        rr48 = prm[:, 248:296]
        so16 = prm[:, 296:312]
        ro16 = prm[:, 312:328]
        rn16 = prm[:, 328:344]
        pst = prm[:, 344:364].rearrange("p (s c) -> p s c", s=2)
        sst = prm[:, 364:370]
        lamin = prm[:, 370:374]
        epsv = prm[:, 374:375]
        nwt = prm[:, 376:424]
        xin = at("x_tiles", WK, [P, NT, D])
        gbc = at("norm_gain", WK + 24, [P, D])
        junk = at("squares", WK + 32, [P, D])
        xs = at("x_normed", WK + 40, [P, 2, D])
        qk = at("qk", WK, [P, 2, NT, GW])
        vs = at("v_new", WK + 12, [P, NT, GW])
        kc = at("k_cache", WK + 18, [P, 2, 2, GW])
        vc = at("v_cache", WK + 26, [P, 2, 2, GW])
        oall = at("o_all", WK + 34, [P, 16, P])
        sq = at("qk_squares", WK + 42, [P, 6 * GW])
        kTc = at("kT_cache", WK + 42, [P, 2, HG, PAST])
        pP = at("p_prompt", WK + 42, [P, 2, 2, 256])
        Wp = at("w_prompt", WK + 46, [P, 256])
        WTp = at("wT_prompt", WK + 47, [P, 2, P])
        qkT = at("qkT_prompt", WK + 50, [P, 2, 512])
        Ps = at("p_sample", WK + 50, [P, 384])
        Ms = at("combine", WK + 51.5, [P, P])
        wTs = at("wT_sample", WK + 52, [P, 3, P])
        qcur = at("q_blockdiag", WK + 53.5, [P, HG, 32])
        qTs = at("qT_sample", WK + 54, [P, HG, P])
        kTn = at("kT_new", WK + 56, [P, HG, P])
        UP = 528
        ub = at("pool_in", WK, [P, 4, UP])
        sA = at("pool_a", WK + 8.25, [P, 4, UP])
        sB = at("pool_b", WK + 16.5, [P, 4, UP])
        dT = at("pool_d", WK + 24.75, [P, 4, T])
        ptok = at("pool_tok", WK + 30.75, [P, NT, W])
        hist = at("pool_hist", WK + 36.75, [P, W])
        wpl = at("w_pool", WK + 38.75, [P, 4, P])
        hh = at("h", WK, [P, NT, D])
        scores = at("scores", MX, [P, NT, D])
        qTk = at("qT_keys", MX + 24, [P, 4, T])
        keyT = at("keysT", MX + 30, [P, 2, P])
        keyr = at("keys_raw", MX + 31, [P, 2, P])
        rT = at("route_T", WK + 48, [P, 3, T])
        onesA = at("onehot_a", WK + 40, [P, 2, 4, P])
        onesB = at("onehot_b", WK + 44, [P, 2, 4, P])
        sc = at("scores_cur", WK + 24, [P, 16, P])
        cand = at("cand", WK + 32, [P, PH, 256])
        eqb = at("eq", WK + 40, [P, PH, TOPK, TOPK])
        tv = at("top_values", WK + 48, [P, 16, 16])
        ti = at("top_index", WK + 49, [P, 16, 16], U32)
        tf = at("top_index_f", WK + 50, [P, 16, 16])
        bv = at("best", WK + 51, [P, PH, 16])
        bi = at("best_index", WK + 51.5, [P, PH, 16], U32)
        bhl = at("best_hl", WK + 52, [P, 2, PH, 16], U32)
        bhf = at("best_hl_f", WK + 53, [P, 2, PH, 16])
        route = at("route", MX + 43, [P, NT, 3, PH * TOPK])
        bst = at("route_stats", WK + 54, [P, 2, PH])
        gsb = at("g_block", WK + 24, [P, 2, P, TB])
        uT = at("u_turned", MX + 24, [P, 2, D])
        aout = at("gelu_out", MX + 40, [P, 2, T])
        zero = at("zeros", WK + 55.5, [P, W])
        gt = at("g_tile", MX, [P, 2, NTB, 8 * TB])
        at_ = at("a_tile", MX + 24, [P, 2, 2, T])
        wt = at("w_tile", MX + 30, [P, 2, 2, T])

        psum = ctx.enter_context(nc.psum_tensor("banks", [P, 8, 512], F32))
        bank = [psum[:, i, :] for i in range(8)]
        pS = [psum[:, 4:6, 0:P], psum[:, 4:6, P:3 * P]]
        Gd = nc.dram_tensor("g_dense", (NTB, P, P * TB), F32, kind="Internal").ap()
        Ad = nc.dram_tensor("a_dense", (P, P, T), F32, kind="Internal").ap()

        names = {}

        def sem(n):
            names[n] = ctx.enter_context(nc.semaphore(n))
            return names[n]

        S_const = sem("s_const")
        x_in = [sem(f"x_in{i}") for i in range(NT)]
        g_in1, g_in2 = sem("gain1_in"), sem("gain2_in")
        raw_ready = [sem("raw_ready0"), sem("raw_ready1")]
        hi_done, lo_done, split_used = sem("hi_done"), sem("lo_done"), sem("split_used")
        n_rt, xs_ready, tr_ready, tr_hi, tr_free = (sem(x) for x in ("n_rt", "xs_ready", "tr_ready", "tr_hi", "tr_free"))
        n_sq = sem("n_sq")
        lam_a, lam_b, lam_c = sem("lam_sums"), sem("lam_exp"), sem("lam_ready")
        proj_ready, proj_free = sem("proj_ready"), sem("proj_free")
        q_sq, q_ss, q_rt, qk_ready = sem("q_sq"), sem("q_ss"), sem("q_rt"), sem("qk_ready")
        kv_stored = sem("kv_stored")
        sT, sTe = sem("s_T"), sem("s_Te")
        p_tr, p_qkT, p_S, p_mx, p_exp, p_W, p_WT, p_WTe, p_o, p_oe = (sem("p_" + x) for x in "tr qkT S mx exp W WT WTe o oe".split())
        cache_in = [sem("cache_in0"), sem("cache_in1")]
        s_q, s_kt, s_kTe, s_S, s_mx, s_exp, s_M, s_w, s_we, s_o, s_oe = (sem("s_" + x) for x in "q kt kTe S mx exp M w we o oe".split())
        o_sq, o_ss, o_rt, o_n, o_t, o_hi, o_lo = (sem("o_" + x) for x in "sq ss rt n t hi lo".split())
        pl_in, pl_zero, pl_tr, pl_up, pl_d, pl_mm, pl_hi, pl_lo = (sem("pl_" + x) for x in "in zero tr up d mm hi lo".split())
        pool_out = sem("pool_out")
        h_in, h_done = sem("h_in"), sem("h_done")
        key_in, key_tr, key_ev, qT_rdy, qT_ev, sc_rdy, sc_ev = (sem(x) for x in "key_in key_tr key_ev qT_rdy qT_ev sc_rdy sc_ev".split())
        cur_ready, cur_free, best_rdy, best_exp, rt_ready, rt_tr, rt_ev = (sem(x) for x in "cur_ready cur_free best_rdy best_exp rt_ready rt_tr rt_ev".split())
        ab_ready, g_mm, g_ev = sem("ab_ready"), sem("g_mm"), sem("g_ev")
        g_store = [sem("g_store0"), sem("g_store1")]
        u_turn, gelu_done = sem("u_turn"), sem("gelu_done")
        a_store = [sem("a_store0"), sem("a_store1")]
        a_in = [sem("a_in0"), sem("a_in1")]
        gg_in = [sem("gt_in0"), sem("gt_in1")]
        w_mult, wh_done, wl_done, z_done, acc_done, y_done = (sem(x) for x in "w_mult wh_done wl_done z_done acc_done y_done".split())
        y_out = sem("y_out")
        g_free, a_free = sem("g_free"), sem("a_free")
        pool_passed, dve_passed = sem("pool_passed"), sem("dve_passed")

        ident = cst[:, C_ID:C_ID + P]
        iota = cst[:, C_IOTA:C_IOTA + P]

        u_v = I["u_tab"][0].rearrange("(r i q) (a d) -> a i q r d", r=4, i=32, q=P, a=4)
        v_v = I["v_tab"][0].rearrange("(p q) d -> p q d", q=P)

        def wait_block(eng, t, blk, n_last):
            if t < NT - 1:
                eng.wait_ge(proj_ready, blk * 2 + (t + 1))
            else:
                eng.wait_ge(split_used, n_last + 3)

        block = ctx.enter_context(nc.Block())

        @block.sync
        def _(sp):
            def load(n, slot, parts, free):
                sp.wait_ge(free[0], free[1])
                for dst, src in parts:
                    sp.dma_start(dst, src).then_inc(raw_ready[slot], 16)

            def weight_step(n, slot, w, kq, cols):
                load(n, slot, [(raw[:, slot, k * W:(k + 1) * W], w[(kq * KQ + k) * P:(kq * KQ + k + 1) * P, cols])
                               for k in range(KQ)], (lo_done, n + 1))

            with sp.Fori(0, NG) as g:
                for s in range(12):
                    blk, kq = divmod(s, 4)
                    weight_step(g * 12 + s, s % 2, I["w_in"][0], kq, ds(g * GW + DPOOL + blk * DATT, W))
            for kq in range(4):
                weight_step(BASE_POOL + kq, kq % 2, I["w_in"][0], kq, ds(0, W))
            with sp.Fori(0, 4) as nb:
                for kq in range(4):
                    weight_step(nb * 4 + (BASE_WOUT + kq), kq % 2, I["w_out"][0], kq, ds(nb * W, W))
            pq = I["w_pq"][0].rearrange("(a b j) n -> a j b n", a=4, b=KC)
            with sp.Fori(0, 4) as nb:
                for kq in range(4):
                    n = nb * 4 + (BASE_WPQ + kq)
                    load(n, kq % 2, [(raw[32 * a:32 * a + 32, kq % 2, :].rearrange("p (b n) -> p b n", b=KQ),
                                      pq[a, :, kq * KQ:(kq + 1) * KQ, ds(nb * W, W)]) for a in range(4)], (lo_done, n + 1))
            with sp.Fori(0, P // 2) as mp:
                for k in range(2):
                    m = mp * 2 + k
                    load(m, k, [(raw[32 * a:32 * a + 32, k, :].rearrange("p (q r d) -> p q r d", r=4, q=1),
                                 u_v[a, :, ds(m, 1), :, :]) for a in range(4)], (u_turn, m + 1))
            sp.wait_ge(a_store[0], 16 * 64)
            sp.wait_ge(a_store[1], 16 * 64)
            sp.wait_ge(g_store[0], 16 * 12)
            sp.wait_ge(g_store[1], 16 * 12)
            for dh in range(2):
                with sp.Fori(0, 8) as it:
                    for s in range(8):
                        v = it * 8 + (dh * 64 + s)
                        n = it * 8 + (dh * 64 + s + BASE_V)
                        slot = s % 2
                        if s % 4 == 0:
                            sp.wait_ge(w_mult, it * 8 + (dh * 64 + s + 4))
                            q16 = it * 2 + s // 4
                            sp.dma_start(gt[:, s // 4, :, :],
                                         Gd.rearrange("b p x -> p b x")[:, :, ds(q16 * P, P)]).then_inc(gg_in[s // 4], 16)
                        sp.wait_ge(w_mult, it * 8 + (dh * 64 + s + 7))
                        i2 = it * 16 + 2 * s
                        sp.dma_start(at_[:, slot, :, :], Ad[ds(i2, 2), :, :].rearrange("q p t -> p q t")).then_inc(a_in[slot], 16)
                        load(n, slot, [(raw[32 * a:32 * a + 32, slot, :].rearrange("p (q d) -> p q d", q=2),
                                        v_v[32 * a:32 * a + 32, ds(i2, 2), dh * 1024:(dh + 1) * 1024]) for a in range(4)],
                             (lo_done, n + 1))
            sp.wait_ge(y_done, 12)
            for t in range(2):
                sp.dma_start(O["y_prompt"][0, t * P:(t + 1) * P, :], hh[:, t, :]).then_inc(y_out, 16)
            sp.dma_start(O["y_sample"].rearrange("b s d -> (b s) d"), hh[:, 2, :]).then_inc(y_out, 16)
            sp.wait_ge(y_out, 48)
            sp.wait_ge(kv_stored, NG * 96)
            sp.wait_ge(pool_out, 16 * 9)

        @block.gpsimd
        def _(pool):
            pool.sem_inc(g_free, 2)
            pool.sem_inc(a_free, 2)

            def loop_wait(sem, value, signal=pool_passed):
                pool.wait_ge(sem, value)
                pool.sem_inc(signal, 1)

            pool.wait_ge(tr_free, 12)
            with pool.Fori(0, NG) as g:
                for b in range(DEC_B):
                    j = b % 2
                    loop_wait(s_o, g * 8 + (b + 1))
                    for t, src in ((kc, "cache_k"), (vc, "cache_v")):
                        v = I[src][0, b] .rearrange("(c p) h e -> p c (h e)", p=P) if src == "cache_v" else \
                            I[src][0, b].rearrange("(c p) h m e -> p c (h m e)", p=P)
                        pool.dma_start(t[:, j, :, :], v[:, :, ds(g * GW, GW)]).then_inc(cache_in[j], 16)
                    if b == 1:
                        loop_wait(qk_ready, g + 1)
                        kp = O["k_prompt"][0, 0].rearrange("s h m e -> s (h m e)")
                        vp = O["v_prompt"][0, 0].rearrange("s h e -> s (h e)")
                        ks = O["k_sample"][0].rearrange("b s h m e -> (b s) (h m e)")
                        vv = O["v_sample"][0].rearrange("b s h e -> (b s) (h e)")
                        for t in range(2):
                            pool.dma_start(kp[t * P:(t + 1) * P, ds(g * GW, GW)], qk[:, 1, t, :]).then_inc(kv_stored, 16)
                            pool.dma_start(vp[t * P:(t + 1) * P, ds(g * GW, GW)], vs[:, t, :]).then_inc(kv_stored, 16)
                        pool.dma_start(ks[:, ds(g * GW, GW)], qk[:, 1, 2, :]).then_inc(kv_stored, 16)
                        pool.dma_start(vv[:, ds(g * GW, GW)], vs[:, 2, :]).then_inc(kv_stored, 16)
            pool.wait_ge(proj_free, 3 + 30)
            pool.dma_start(O["pool_prompt"][0, 0], ptok[P - HIST:P, 1, :]).then_inc(pool_out, 16)
            for b in range(DEC_B):
                pool.dma_start(O["pool_sample"][0, b], ptok[16 * b + 1:16 * b + 16, 2, :]).then_inc(pool_out, 16)
            def store_gelu(m, k):
                loop_wait(gelu_done, m + 3)
                pool.dma_start(Ad[ds(m, 1), :, :].rearrange("o p x -> (o p) x"), aout[:, k, :]).then_inc(a_store[k], 16)

            def stored_gelu(mp):
                for k in range(2):
                    loop_wait(a_store[k], mp * 16 + 16, a_free)

            with pool.Fori(0, U_ROUTE // 2) as mp:
                for k in range(2):
                    store_gelu(mp * 2 + k, k)
                stored_gelu(mp)
            with pool.Fori(0, NTB // 2) as it:
                for sl in range(2):
                    for k in range(2):
                        store_gelu(it * 4 + (U_ROUTE + 2 * sl + k), k)
                    stored_gelu(it * 2 + (U_ROUTE // 2 + sl))
                    loop_wait(g_ev, it * 8 + (4 * sl + 4 + 2))
                    pool.dma_start(Gd[ds(it * 2 + sl, 1), :, :].rearrange("o p x -> (o p) x"),
                                   gsb[:, sl, :, :].rearrange("p a b -> p (a b)")).then_inc(g_store[sl], 16)
                    loop_wait(g_store[sl], it * 16 + 16, g_free)
            with pool.Fori(0, U_REST // 2) as mp:
                for k in range(2):
                    store_gelu(mp * 2 + (U_ROUTE + U_DENSE + k), k)
                stored_gelu(mp + (U_ROUTE + U_DENSE) // 2)

        @block.scalar
        def _(act):
            A = nc.scalar.activation
            for one in (p_oe, s_kTe, s_exp, s_we, s_oe, rt_ev):
                act.sem_inc(one, 1)
            act.sem_inc(gelu_done, 2)
            act.sem_inc(g_ev, 2)
            act.dma_start(cst[:, :], I["cst"]).then_inc(S_const, 16)
            for m, nme in enumerate(("q_norm_g", "k_norm_g")):
                act.dma_start(gqk[:, m, :], I[nme].broadcast_to([P, HD])).then_inc(S_const, 16)
            act.dma_start(pscale, I["pool_scale"][0].rearrange("(g c) -> c g", c=P)).then_inc(S_const, 16)
            act.dma_start(subg, I["subln_g"].rearrange("o c -> c o")).then_inc(S_const, 16)
            for m, nme in enumerate(("lambda_q1", "lambda_k1", "lambda_q2", "lambda_k2")):
                act.dma_start(xs[:, 1, m * HD:(m + 1) * HD], I[nme].broadcast_to([P, HD])).then_inc(S_const, 16)
            xp = [I["x_prompt"][0, 0:P, :], I["x_prompt"][0, P:2 * P, :], I["x_sample"].rearrange("b s d -> (b s) d")]
            for t in range(NT):
                act.dma_start(xin[:, t, :], xp[t]).then_inc(x_in[t], 16)
            act.dma_start(gbc[:, :], I["norm1_g"].broadcast_to([P, D])).then_inc(g_in1, 16)

            def split_hi(n, slot, src=None):
                if src is None:
                    act.wait_ge(raw_ready[slot], n * 32 + (64 - 32 * (slot % 2)))
                act.wait_ge(split_used, n + 1)
                A(ringH[:, slot, :], raw[:, slot, :], ACT.Copy).then_inc(hi_done, 1)

            def norm_part(p, src, ready):
                for t in range(NT):
                    act.wait_ge(*ready(t))
                    A(junk[:, :], src[:, t, :], ACT.Square, accum_out=ssx[:, t:t + 1]).then_inc(n_sq, 1)
                    act.wait_ge(n_sq, p * 3 + t + 1)
                A(rtx, ssx, ACT.Sqrt, scale=1.0 / D, bias=epsv).then_inc(n_rt, 1)
                for t in range(NT):
                    for q in range(4):
                        n = p * 12 + t * 4 + q
                        act.wait_ge(tr_ready, n + 1)
                        A(xTh[:, 4 * q:4 * q + 4, t * P:(t + 1) * P],
                          bank[3 + q][:, :].rearrange("p (k t) -> p k t", k=4), ACT.Copy).then_inc(tr_hi, 1)

            act.wait_ge(S_const, 16 * 9)
            act.wait_ge(z_done, 1)
            act.wait_ge(lam_a, 1)
            A(lame, lamin[:, 0:2], ACT.Exp).then_inc(lam_b, 1)
            norm_part(0, xin, lambda t: (x_in[t], 16))

            with act.Fori(0, NG) as g:
                def evac_block(blk):
                    dst = qk[:, blk, :, :] if blk < 2 else vs[:, :, :]
                    for t in range(NT):
                        wait_block(act, t, g * 3 + blk, g * 12 + (4 * blk + 3))
                        A(dst[:, t, :], bank[t][:, :], ACT.Copy).then_inc(proj_free, 1)

                for s in range(12):
                    split_hi(g * 12 + s, s % 2)
                    if s == 4:
                        evac_block(0)
                    if s == 8:
                        evac_block(1)
                evac_block(2)
                act.wait_ge(proj_free, g * 9 + (3 + 6))
                A(sq[:, :], qk[:, :, :, :].rearrange("p a b c -> p (a b c)"), ACT.Square).then_inc(q_sq, 1)
                act.wait_ge(q_ss, g + 1)
                A(rt48, ss48, ACT.Sqrt, scale=1.0 / HD, bias=epsv).then_inc(q_rt, 1)
                act.wait_ge(sT, g * 2 + 2)
                A(qTs[:, :, :].rearrange("p h t -> p (h t)"), bank[5][:, :], ACT.Copy).then_inc(sTe, 1)
                A(kTn[:, :, :].rearrange("p h t -> p (h t)"), bank[6][:, :], ACT.Copy).then_inc(sTe, 1)

                def p_evac(h):
                    act.wait_ge(p_tr, g * 4 + (h + 1))
                    A(qkT[:, h % 2, :], bank[3][:, :], ACT.Copy).then_inc(p_qkT, 1)

                def p_exps(m):
                    qt = m % 2
                    nk = P * (qt + 1)
                    act.wait_ge(p_mx, g * 8 + (m // 2 * 2 + 2))
                    for c in range(2):
                        last = A(pP[:, qt, c, 0:nk], pS[qt][:, c, :], ACT.Exp,
                                 scale=QS, bias=pst[:, qt, 2 + c:3 + c], accum_out=pst[:, qt, 4 + c:5 + c])
                    last.then_inc(p_exp, 1)

                def p_out(m):
                    nkt = m % 2 + 1
                    act.wait_ge(p_WT, g * 8 + (m + 2))
                    A(WTp[:, 0:nkt, :].rearrange("p a b -> p (a b)"), bank[6][:, 0:nkt * P], ACT.Copy).then_inc(p_WTe, 1)
                    act.wait_ge(p_o, g * 8 + (m + 1))
                    A(oall[:, m, :], bank[7][:, 0:P], ACT.Copy).then_inc(p_oe, 1)

                p_evac(0)
                p_exps(0)
                p_exps(1)
                for h in range(HG):
                    if h + 1 < HG:
                        p_evac(h + 1)
                    for qt in range(2):
                        p_out(2 * h + qt)
                    if h + 1 < HG:
                        p_exps(2 * h + 2)
                        p_exps(2 * h + 3)

                def s_kev(b):
                    act.wait_ge(s_kt, g * 8 + (b + 1))
                    for i in range(2):
                        last = A(kTc[:, b % 2, 2 * i:2 * i + 2, :].rearrange("p h k -> p (h k)"), bank[3 + i][:, :], ACT.Copy)
                    last.then_inc(s_kTe, 1)

                s_kev(0)
                for b in range(DEC_B):
                    if b + 1 < DEC_B:
                        s_kev(b + 1)
                    act.wait_ge(s_mx, g * 8 + (b + 1))
                    act.wait_ge(s_w, g * 8 + (b + 1))
                    A(Ps[:, :], bank[5][:, 0:384], ACT.Exp, scale=QS, bias=sst[:, 1:2],
                      accum_out=sst[:, 2:3]).then_inc(s_exp, 1)
                    act.wait_ge(s_w, g * 8 + (b + 2))
                    A(wTs[:, :, :].rearrange("p a b -> p (a b)"), bank[6][:, 0:384], ACT.Copy).then_inc(s_we, 1)
                    act.wait_ge(s_o, g * 8 + (b + 3))
                    A(oall[:, 8 + b, :], bank[7][:, 0:P], ACT.Copy).then_inc(s_oe, 1)
                act.wait_ge(s_oe, g * 8 + 9)
                A(sq[:, 0:D], oall[:, :, :].rearrange("p a b -> p (a b)"), ACT.Square).then_inc(o_sq, 1)
                act.wait_ge(o_ss, g + 1)
                A(ro16, so16, ACT.Sqrt, scale=1.0 / VD, bias=epsv).then_inc(o_rt, 1)
                for i in range(4):
                    act.wait_ge(o_t, g * 4 + (i + 1))
                    if i < 2:
                        A(mixTh[:, ds(g * 4 + (4 + 2 * i), 2), 0:SEQ], bank[3 + i][:, :].rearrange("p (h t) -> p h t", h=2),
                          ACT.Copy, scale=subg).then_inc(o_hi, 1)
                    else:
                        for b in range(4):
                            c0 = SEQ + 16 * (4 * (i - 2) + b)
                            last = A(mixTh[:, ds(g * 4 + 4, 4), c0:c0 + 16],
                                     bank[3 + i][:, b * P:(b + 1) * P].rearrange("p (h t) -> p h t", h=4)[:, :, 0:16],
                                     ACT.Copy, scale=subg)
                        last.then_inc(o_hi, 1)
                act.wait_ge(kv_stored, g * 96 + 96)

            for kq in range(4):
                split_hi(BASE_POOL + kq, kq % 2)
            act.wait_ge(o_lo, 13)
            act.wait_ge(kv_stored, NG * 96)
            act.dma_start(hist[0:DEC_B * HIST, :], I["state_pool"][0].rearrange("b j c -> (b j) c")).then_inc(pl_in, 16)
            act.dma_start(wpl[:, :, :], I["w_pool"][0].rearrange("g c d -> c g d")).then_inc(pl_in, 16)
            for t in range(NT):
                wait_block(act, t, 9, BASE_POOL + 3)
                A(ptok[:, t, :], bank[t][:, :], ACT.Copy).then_inc(proj_free, 1)
            split_hi(BASE_WOUT, 0)
            split_hi(BASE_WOUT + 1, 1)
            act.wait_ge(pl_zero, 1)
            for gg in range(4):
                act.wait_ge(pl_tr, gg + 1)
                A(ub[:, gg, 16:272], bank[3 + gg][:, 0:256], ACT.Copy)
                A(ub[:, gg, 272:528].rearrange("p (b s) -> p b s", b=8)[:, :, 16:32],
                  bank[3 + gg][:, 256:384].rearrange("p (b s) -> p b s", b=8), ACT.Copy).then_inc(pl_up, 1)
            act.wait_ge(pl_tr, 5)
            for gg in range(4):
                last = A(ub[:, gg, 272:528].rearrange("p (b s) -> p b s", b=8)[:, :, 1:16],
                         bank[7][:, gg * 120:(gg + 1) * 120].rearrange("p (b s) -> p b s", b=8), ACT.Copy)
            last.then_inc(pl_up, 1)
            for gg in range(4):
                act.wait_ge(pl_mm, gg + 1)
                A(mixTh[:, gg, :], bank[3 + gg][:, 0:T], ACT.Copy, scale=pscale[:, gg:gg + 1]).then_inc(pl_hi, 1)
            act.wait_ge(pl_lo, 4)
            act.wait_ge(pool_out, 16 * 9)
            for t in range(NT):
                act.dma_start(hh[:, t, :], xp[t]).then_inc(h_in, 16)
            act.dma_start(gbc[:, :], I["norm2_g"].broadcast_to([P, D])).then_inc(g_in2, 16)
            for s in range(2, 16):
                split_hi(BASE_WOUT + s, s % 2)
            norm_part(1, hh, lambda t: (h_done, 10 + t))
            act.dma_start(keyr[:, :, :], I["sub_keys"][0].rearrange("c k d -> k c d")).then_inc(key_in, 16)
            act.wait_ge(key_tr, 1)
            A(keyT[:, :, :].rearrange("p c k -> p (c k)"), bank[7][:, 0:256], ACT.Copy).then_inc(key_ev, 1)

            def score_evac(nb):
                for t in range(NT):
                    act.wait_ge(sc_rdy, nb * 3 + t + 1)
                    A(scores[:, t, nb * W:(nb + 1) * W], bank[4 + t][:, :], ACT.Copy).then_inc(sc_ev, 1)

            for nb in range(4):
                for kq in range(4):
                    split_hi(BASE_WPQ + nb * 4 + kq, kq % 2)
                    if kq == 1 and nb > 0:
                        score_evac(nb - 1)
                for sub in range(4):
                    if sub < 3:
                        act.wait_ge(qT_rdy, nb * 3 + sub + 1)
                    else:
                        act.wait_ge(split_used, BASE_WPQ + nb * 4 + 3 + 3)
                    A(qTk[:, sub, :], bank[sub][:, 0:T], ACT.Copy).then_inc(qT_ev, 1)
            score_evac(3)

            act.wait_ge(sc_ev, 12)

            def u_hi(m, k):
                act.wait_ge(u_turn, m + 3)
                act.wait_ge(split_used, m + (BASE_U + 1))
                A(ringH[:, k, :].rearrange("p (b r i) -> p r b i", b=KC, r=4),
                  uT[:, k, :].rearrange("p (r b i) -> p r b i", r=4, b=KC), ACT.Copy).then_inc(hi_done, 1)

            def gelu(m, k):
                act.wait_ge(split_used, m + (BASE_U + 3))
                act.wait_ge(a_free, m + 1)
                A(aout[:, k, :], bank[k][:, 0:T], ACT.Gelu_apprx_tanh).then_inc(gelu_done, 1)

            u_hi(0, 0)
            with act.Fori(0, NT) as t:
                act.wait_ge(cur_free, t + 1)
                A(sc[:, :, :].rearrange("p a b -> p (a b)"), scores[:, ds(t, 1), :].rearrange("p o x -> p (o x)"), ACT.Copy).then_inc(cur_ready, 1)
                for j in range(N_PARTS):
                    m = t * N_PARTS + j
                    u_hi(m + 1, (j + 1) % 2)
                    gelu(m, j % 2)
                    if j == 13:
                        act.wait_ge(best_rdy, t + 1)
                        A(bv[:, :, :], bv[:, :, :], ACT.Exp).then_inc(best_exp, 1)
            act.wait_ge(rt_tr, 3)
            A(rT[:, :, :].rearrange("p a t -> p (a t)")[:, 0:2 * T].rearrange("p (c t) -> p c t", c=2),
              psum[:, 4:6, 0:T], ACT.Copy)
            A(rT[:, 2, :], bank[6][:, 0:T], ACT.Copy).then_inc(rt_ev, 1)
            with act.Fori(0, NTB // 2) as it:
                for s in range(4):
                    m = it * 4 + (U_ROUTE + s)
                    u_hi(m + 1, (s + 1) % 2)
                    gelu(m, s % 2)
                    sl = s // 2
                    if s % 2 == 0:
                        act.wait_ge(g_free, it * 2 + (sl + 1))
                    for qd in range(2 * s, 2 * s + 2):
                        act.wait_ge(g_mm, it * 8 + (qd + 3))
                        c0 = 4 * (qd % 4)
                        A(gsb[:, sl, :, c0:c0 + 4].rearrange("p i t -> p t i"),
                          bank[6 + qd % 2][:, :].rearrange("p (t i) -> p t i", t=4), ACT.Copy).then_inc(g_ev, 1)
            with act.Fori(0, U_REST // 2 - 1) as mp:
                for k in range(2):
                    m = mp * 2 + (U_ROUTE + U_DENSE + k)
                    u_hi(m + 1, (k + 1) % 2)
                    gelu(m, k)
            u_hi(P - 1, 1)
            gelu(P - 2, 0)
            gelu(P - 1, 1)

            for dh in range(2):
                with act.Fori(0, 8) as it:
                    for s in range(8):
                        split_hi_v = it * 8 + (BASE_V + dh * 64 + s)
                        split_hi(split_hi_v, s % 2)
                        act.wait_ge(w_mult, it * 8 + (dh * 64 + s + 9))
                        A(xTh[:, 2 * (s % 2):2 * (s % 2) + 2, :], wt[:, s % 2, :, :], ACT.Copy).then_inc(wh_done, 1)

        @block.vector
        def _(dve):
            V = nc.vector

            def drain():
                dve.drain()

            def refined_rsqrt(r, root, total, tmp, n):
                V.reciprocal(r, root)
                V.tensor_scalar(total, total, 1.0 / n, EPS, ALU.mult, ALU.add)
                drain()
                V.tensor_tensor(tmp, r, r, ALU.mult)
                drain()
                V.tensor_tensor(tmp, tmp, total, ALU.mult)
                drain()
                V.tensor_scalar(tmp, tmp, -0.5, 1.5, ALU.mult, ALU.add)
                drain()
                V.tensor_tensor(r, r, tmp, ALU.mult)
                drain()

            for one in (o_lo, cur_free):
                dve.sem_inc(one, 1)
            dve.sem_inc(lo_done, 2)
            V.memset(epsv, EPS).then_inc(z_done, 1)
            dve.wait_ge(S_const, 16 * 9)
            lv = xs[:, 1, 0:4 * HD].rearrange("p (m c e) -> p m c e", m=2, c=2)
            V.tensor_tensor(xs[:, 1, 512:640].rearrange("p (m e) -> p m e", m=2), lv[:, :, 0, :], lv[:, :, 1, :], ALU.mult)
            drain()
            V.tensor_reduce(lamin[:, 0:2], xs[:, 1, 512:640].rearrange("p (m e) -> p m e", m=2), AX.X, ALU.add).then_inc(lam_a, 1)
            dve.wait_ge(lam_b, 1)
            V.tensor_tensor(lamv, lame[:, 0:1], lame[:, 1:2], ALU.subtract)
            drain()
            V.tensor_scalar(lamv, lamv, LAM_INIT, None, ALU.add)
            drain()
            V.tensor_scalar(cvt, cst[:, C_CV + 1:C_CV + 2], lamv, None, ALU.mult)
            drain()
            V.tensor_tensor(cvec, cst[:, C_CV:C_CV + 1], cvt, ALU.subtract)
            drain()

            def split_lo(n, slot):
                dve.wait_ge(hi_done, n + 1)
                V.tensor_tensor(ringL[:, slot, :], raw[:, slot, :], ringH[:, slot, :].bitcast(F32), ALU.subtract).then_inc(lo_done, 1)

            def norm_part(p, src, gain):
                dve.wait_ge(n_rt, p + 1)
                refined_rsqrt(rrx, rtx, ssx, nwt[:, 0:3], D)
                dve.wait_ge(*gain)

                def scaled(t):
                    if t == 2:
                        dve.wait_ge(tr_ready, p * 12 + 4)
                    if p == 0:
                        V.scalar_tensor_tensor(out=xs[:, t % 2, :], in0=src[:, t, :], scalar=rrx[:, t:t + 1], in1=gbc[:, :],
                                               op0=ALU.mult, op1=ALU.mult).then_inc(xs_ready, 1)
                    else:
                        for a in range(4):
                            last = V.scalar_tensor_tensor(
                                out=xs[:, t % 2, :].rearrange("p (b a j) -> p a b j", b=KC, a=4)[:, a, :, :],
                                in0=src[:, t, a * 512:(a + 1) * 512].rearrange("p (b j) -> p b j", b=KC), scalar=rrx[:, t:t + 1],
                                in1=gbc[:, a * 512:(a + 1) * 512].rearrange("p (b j) -> p b j", b=KC),
                                op0=ALU.mult, op1=ALU.mult)
                        last.then_inc(xs_ready, 1)

                def lo(t):
                    for q in range(4):
                        n = p * 12 + t * 4 + q
                        dve.wait_ge(tr_hi, n + 1)
                        V.tensor_tensor(xTl[:, 4 * q:4 * q + 4, t * P:(t + 1) * P],
                                        bank[3 + q][:, :].rearrange("p (k t) -> p k t", k=4),
                                        xTh[:, 4 * q:4 * q + 4, t * P:(t + 1) * P].bitcast(F32), ALU.subtract).then_inc(tr_free, 1)

                scaled(0)
                scaled(1)
                lo(0)
                scaled(2)
                lo(1)
                lo(2)

            norm_part(0, xin, (g_in1, 16))
            dve.wait_ge(tr_free, 12)

            with dve.Fori(0, NG) as g:
                for s in range(12):
                    split_lo(g * 12 + s, s % 2)
                dve.wait_ge(q_sq, g + 1)
                V.tensor_reduce(ss48, sq[:, :].rearrange("p (a e) -> p a e", e=HD), AX.X, ALU.add).then_inc(q_ss, 1)
                dve.wait_ge(q_rt, g + 1)
                refined_rsqrt(rr48, rt48, ss48, nwt[:, 0:48], HD)
                q3 = qk[:, :, :, :].rearrange("p m t (h e) -> p (m t h) e", e=HD)
                V.tensor_tensor(q3, q3, rr48.unsqueeze(2).broadcast_to([P, 48, HD]), ALU.mult)
                drain()
                for m in range(2):
                    qm = qk[:, m, :, :].rearrange("p t (h e) -> p (t h) e", e=HD)
                    V.tensor_tensor(qm, qm, gqk[:, m:m + 1, :].broadcast_to([P, 24, HD]), ALU.mult)
                drain()
                rope = cst[:, C_ROPE:C_PM].rearrange("p (t c e) -> p t c e", t=NT, c=2)
                tmp = sq[:, 0:4 * 2 * 192].rearrange("p (k m t h e) -> p k m t h e", k=4, m=2, t=NT, h=8)
                for m in range(2):
                    qh = qk[:, m, :, :].rearrange("p t (h e) -> p t h e", e=HD)
                    cos = rope[:, :, 0:1, :].broadcast_to([P, NT, 8, 8])
                    sin = rope[:, :, 1:2, :].broadcast_to([P, NT, 8, 8])
                    x1, x2 = qh[:, :, :, 0:8], qh[:, :, :, 8:16]
                    for k, (a, b) in enumerate(((x1, cos), (x2, sin), (x2, cos), (x1, sin))):
                        V.tensor_tensor(tmp[:, k, m], a, b, ALU.mult)
                drain()
                for m in range(2):
                    qh = qk[:, m, :, :].rearrange("p t (h e) -> p t h e", e=HD)
                    V.tensor_tensor(qh[:, :, :, 0:8], tmp[:, 0, m], tmp[:, 1, m], ALU.subtract)
                    last = V.tensor_tensor(qh[:, :, :, 8:16], tmp[:, 2, m], tmp[:, 3, m], ALU.add)
                last.then_inc(qk_ready, 1)

                pm = cst[:, C_PM:C_SM]

                def p_max(m):
                    qt = m % 2
                    nk = P * (qt + 1)
                    dve.wait_ge(p_S, g * 4 + (m // 2 + 1))
                    s2 = pS[qt]
                    V.tensor_tensor(s2[:, :, nk - 64:nk], s2[:, :, nk - 64:nk], pm.unsqueeze(1).broadcast_to([P, 2, 64]), ALU.add)
                    drain()
                    V.tensor_reduce(pst[:, qt, 0:2], s2[:, :, 0:nk], AX.X, ALU.max)
                    drain()
                    V.tensor_scalar(pst[:, qt, 2:4], pst[:, qt, 0:2], -QS, None, ALU.mult).then_inc(p_mx, 1)

                def p_comb(m):
                    qt = m % 2
                    nk = P * (qt + 1)
                    dve.wait_ge(p_exp, g * 8 + (m + 1))
                    V.reciprocal(pst[:, qt, 6:8], pst[:, qt, 4:6])
                    drain()
                    V.tensor_tensor(pst[:, qt, 8:9], pst[:, qt, 7:8], lamv, ALU.mult)
                    drain()
                    dve.wait_ge(p_WT, g * 8 + (m + 1))
                    V.tensor_scalar(Wp[:, 0:nk], pP[:, qt, 1, 0:nk], pst[:, qt, 8:9], None, ALU.mult)
                    drain()
                    V.scalar_tensor_tensor(out=Wp[:, 0:nk], in0=pP[:, qt, 0, 0:nk], scalar=pst[:, qt, 6:7], in1=Wp[:, 0:nk],
                                           op0=ALU.mult, op1=ALU.subtract).then_inc(p_W, 1)

                p_max(0)
                p_max(1)
                for h in range(HG):
                    p_comb(2 * h)
                    p_comb(2 * h + 1)
                    if h + 1 < HG:
                        p_max(2 * h + 2)
                        p_max(2 * h + 3)

                def q_diag(b):
                    dve.wait_ge(s_S, g * 8 + (b + 1))
                    V.tensor_copy(qcur[0:64, :, 0:16], qTs[0:64, :, 16 * b:16 * b + 16])
                    V.tensor_copy(qcur[64:128, :, 16:32], qTs[64:128, :, 16 * b:16 * b + 16]).then_inc(s_q, 1)

                V.memset(qcur[:, :, :], 0.0)
                drain()
                dve.wait_ge(sTe, g * 2 + 2)
                q_diag(0)
                for b in range(DEC_B):
                    dve.wait_ge(s_S, g * 8 + (b + 2))
                    V.tensor_tensor(bank[5][:, 256:384], bank[5][:, 256:384], cst[:, C_SM + 112 - 16 * b:C_SM + 240 - 16 * b], ALU.add)
                    drain()
                    V.tensor_reduce(sst[:, 0:1], bank[5][:, 0:384], AX.X, ALU.max)
                    drain()
                    V.tensor_scalar(sst[:, 1:2], sst[:, 0:1], -QS, None, ALU.mult).then_inc(s_mx, 1)
                    if b + 1 < DEC_B:
                        q_diag(b + 1)
                    dve.wait_ge(s_exp, g * 8 + (b + 2))
                    V.reciprocal(sst[:, 3:4], sst[:, 2:3])
                    drain()
                    V.tensor_scalar(Ms[:, :], cst[:, C_SEL:C_SEL + P], sst[:, 3:4], cvec, ALU.mult, ALU.mult).then_inc(s_M, 1)
                dve.wait_ge(o_sq, g + 1)
                V.tensor_reduce(so16, sq[:, 0:D].rearrange("p (a e) -> p a e", e=VD), AX.X, ALU.add).then_inc(o_ss, 1)
                dve.wait_ge(o_rt, g + 1)
                refined_rsqrt(rn16, ro16, so16, nwt[:, 0:16], VD)
                V.tensor_scalar(rn16, rn16, 1.0 - LAM_INIT, None, ALU.mult)
                drain()
                V.tensor_tensor(oall[:, :, :], oall[:, :, :], rn16.unsqueeze(2).broadcast_to([P, 16, VD]), ALU.mult).then_inc(o_n, 1)
                for i in range(4):
                    dve.wait_ge(o_hi, g * 4 + (i + 1))
                    if i < 2:
                        mh = mixTh[:, ds(g * 4 + (4 + 2 * i), 2), 0:SEQ]
                        ml = mixTl[:, ds(g * 4 + (4 + 2 * i), 2), 0:SEQ]
                        V.scalar_tensor_tensor(out=ml, in0=bank[3 + i][:, :].rearrange("p (h t) -> p h t", h=2), scalar=subg,
                                               in1=mh.bitcast(F32), op0=ALU.mult, op1=ALU.subtract).then_inc(o_lo, 1)
                    else:
                        for b in range(4):
                            c0 = SEQ + 16 * (4 * (i - 2) + b)
                            last = V.scalar_tensor_tensor(
                                out=mixTl[:, ds(g * 4 + 4, 4), c0:c0 + 16],
                                in0=bank[3 + i][:, b * P:(b + 1) * P].rearrange("p (h t) -> p h t", h=4)[:, :, 0:16], scalar=subg,
                                in1=mixTh[:, ds(g * 4 + 4, 4), c0:c0 + 16].bitcast(F32), op0=ALU.mult, op1=ALU.subtract)
                        last.then_inc(o_lo, 1)

            for kq in range(4):
                split_lo(BASE_POOL + kq, kq % 2)
            dve.wait_ge(kv_stored, NG * 96)
            dve.wait_ge(o_lo, 13)
            V.memset(ub[:, :, :], 0.0).then_inc(pl_zero, 1)
            split_lo(BASE_WOUT, 0)
            split_lo(BASE_WOUT + 1, 1)
            dve.wait_ge(pl_up, 5)
            src, w = ub, 1
            dsts = [sA, sB, sA, sB]
            for g in range(4):
                lo_c = 2 * w - 1
                V.tensor_tensor(dsts[g][:, g:4, lo_c:UP], src[:, g:4, lo_c:UP], src[:, g:4, lo_c - w:UP - w], ALU.add)
                drain()
                src, w = dsts[g], 2 * w
            inv = cst[:, C_INV:C_INV + 64].rearrange("p (g t) -> p g t", g=4)
            for g in range(4):
                wn = 1.0 / 2 ** (g + 1)
                V.scalar_tensor_tensor(out=dT[:, g, 16:SEQ], in0=dsts[g][:, g, 32:272], scalar=wn, in1=ub[:, g, 32:272],
                                       op0=ALU.mult, op1=ALU.subtract)
                V.scalar_tensor_tensor(out=dT[:, g, SEQ:T].rearrange("p (b s) -> p b s", b=8),
                                       in0=dsts[g][:, g, 272:528].rearrange("p (b s) -> p b s", b=8)[:, :, 16:32], scalar=wn,
                                       in1=ub[:, g, 272:528].rearrange("p (b s) -> p b s", b=8)[:, :, 16:32],
                                       op0=ALU.mult, op1=ALU.subtract)
                V.tensor_tensor(dT[:, g, 0:16], dsts[g][:, g, 16:32], inv[:, g, :], ALU.mult)
                drain()
                V.tensor_tensor(dT[:, g, 0:16], dT[:, g, 0:16], ub[:, g, 16:32], ALU.subtract).then_inc(pl_d, 1)
            for gg in range(4):
                dve.wait_ge(pl_hi, gg + 1)
                V.scalar_tensor_tensor(out=mixTl[:, gg, :], in0=bank[3 + gg][:, 0:T], scalar=pscale[:, gg:gg + 1],
                                       in1=mixTh[:, gg, :].bitcast(F32), op0=ALU.mult, op1=ALU.subtract).then_inc(pl_lo, 1)

            def add_residual(nb):
                for t in range(NT):
                    wait_block(dve, t, 10 + nb, BASE_WOUT + 4 * nb + 3)
                    hs = hh[:, t, nb * W:(nb + 1) * W]
                    V.tensor_tensor(hs, bank[t][:, :], hs, ALU.add).then_inc(h_done, 1)

            for s in range(2, 16):
                split_lo(BASE_WOUT + s, s % 2)
                if s % 4 == 0:
                    dve.wait_ge(h_in, 48)
                    add_residual(s // 4 - 1)
            add_residual(3)
            norm_part(1, hh, (g_in2, 16))
            for s in range(16):
                split_lo(BASE_WPQ + s, s % 2)
            dve.drain().then_inc(u_turn, 2)

            def turn(m, k):
                dve.wait_ge(raw_ready[k], m * 32 + (64 * (BASE_U // 2 + 1) - 32 * k))
                dve.wait_ge(lo_done, m + (BASE_U + 1))
                V.transpose(uT[:, k, :], raw[:, k, :]).then_inc(u_turn, 1)

            def u_lo(m, k):
                dve.wait_ge(hi_done, m + (BASE_U + 1))
                V.tensor_tensor(ringL[:, k, :].rearrange("p (b r i) -> p r b i", b=KC, r=4),
                                uT[:, k, :].rearrange("p (r b i) -> p r b i", r=4, b=KC),
                                ringH[:, k, :].bitcast(F32).rearrange("p (b r i) -> p r b i", b=KC, r=4), ALU.subtract).then_inc(lo_done, 1)

            tvh = tv[:, :, :].rearrange("p (h c) k -> p h c k", c=2)
            tfh = tf[:, :, :].rearrange("p (h c) k -> p h c k", c=2)
            full = [P, PH, TOPK, TOPK]

            def route_index(t, c, part):
                if part == 0:
                    V.tensor_tensor(eqb[:, :, :, :], bhf[:, c].unsqueeze(3).broadcast_to(full),
                                    cst[:, C_IOTA:C_IOTA + 16].unsqueeze(1).unsqueeze(1).broadcast_to(full), ALU.is_equal)
                elif part == 1:
                    V.tensor_tensor(eqb[:, :, :, :], eqb[:, :, :, :], tfh[:, :, c:c + 1, :].broadcast_to(full), ALU.mult)
                else:
                    V.tensor_reduce(route[:, ds(t, 1), 1 + c, :].rearrange("p o (h k) -> p (o h) k", h=PH), eqb[:, :, :, :], AX.X, ALU.add)

            def routing_part(t, j):
                if j == 0:
                    dve.wait_ge(cur_ready, t + 1)
                    dve.sem_inc(dve_passed, 1)
                if j in (0, 3):
                    k = slice(0, 8) if j == 0 else slice(8, 16)
                    for i in range(16):
                        V.max(tv[:, i, k], sc[:, i, :])
                elif j in (1, 4):
                    k = slice(0, 8) if j == 1 else slice(8, 16)
                    for i in range(16):
                        V.max_index(ti[:, i, k], tv[:, i, k], sc[:, i, :])
                elif j == 2:
                    for i in range(16):
                        V.match_replace(sc[:, i, :], tv[:, i, 0:8], sc[:, i, :], NEG)
                elif j == 5:
                    V.tensor_copy(tf[:, :, :], ti[:, :, :]).then_inc(cur_free, 1)
                    V.tensor_tensor(cand[:, :, :].rearrange("p h (a b) -> p h a b", a=TOPK), tvh[:, :, 0, :].unsqueeze(3).broadcast_to(full),
                                    tvh[:, :, 1:2, :].broadcast_to(full), ALU.add)
                elif j in (6, 9):
                    k = slice(0, 8) if j == 6 else slice(8, 16)
                    for h in range(PH):
                        V.max(bv[:, h, k], cand[:, h, :])
                elif j in (7, 10):
                    k = slice(0, 8) if j == 7 else slice(8, 16)
                    for h in range(PH):
                        V.max_index(bi[:, h, k], bv[:, h, k], cand[:, h, :])
                elif j == 8:
                    for h in range(PH):
                        V.match_replace(cand[:, h, :], bv[:, h, 0:8], cand[:, h, :], NEG)
                elif j == 11:
                    V.tensor_copy(bst[:, 0, :], bv[:, :, 0])
                    V.tensor_scalar(bhl[:, 0], bi[:, :, :], 4, None, ALU.logical_shift_right)
                    V.tensor_scalar(bhl[:, 1], bi[:, :, :], 15, None, ALU.bitwise_and)
                    drain()
                    V.tensor_tensor(bv[:, :, :], bv[:, :, :], bst[:, 0, :].unsqueeze(2).broadcast_to([P, PH, TOPK]), ALU.subtract).then_inc(best_rdy, 1)
                    V.tensor_copy(bhf[:, :, :, :], bhl[:, :, :, :])
                elif j < 17:
                    route_index(t, (j - 12) // 3, (j - 12) % 3)
                else:
                    route_index(t, 1, 2)
                    dve.wait_ge(best_exp, t + 1)
                    V.tensor_reduce(bst[:, 0, :], bv[:, :, :], AX.X, ALU.add)
                    drain()
                    V.reciprocal(bst[:, 1, :], bst[:, 0, :])
                    drain()
                    V.tensor_tensor(route[:, ds(t, 1), 0, :].rearrange("p o (h k) -> p (o h) k", h=PH), bv[:, :, :],
                                    bst[:, 1, :].unsqueeze(2).broadcast_to([P, PH, TOPK]), ALU.mult).then_inc(rt_ready, 1)
                drain()

            def one_hots(it, qd):
                dve.wait_ge(g_mm, it * 8 + (qd + 1))
                for i in range(4):
                    tk = it * 32 + (qd * 4 + i)
                    V.tensor_scalar(onesA[:, qd % 2, i, :], iota, rT[:, 1, ds(tk, 1)], rT[:, 0, ds(tk, 1)], ALU.is_equal, ALU.mult)
                    last = V.tensor_scalar(onesB[:, qd % 2, i, :], iota, rT[:, 2, ds(tk, 1)], None, ALU.is_equal)
                last.then_inc(ab_ready, 1)

            dve.wait_ge(sc_rdy, 12)
            turn(0, 0)
            with dve.Fori(0, NT) as t:
                for j in range(N_PARTS):
                    m = t * N_PARTS + j
                    turn(m + 1, (j + 1) % 2)
                    u_lo(m, j % 2)
                    routing_part(t, j)
            dve.wait_ge(rt_ev, 2)
            with dve.Fori(0, NTB // 2) as it:
                for s in range(4):
                    m = it * 4 + (U_ROUTE + s)
                    turn(m + 1, (s + 1) % 2)
                    u_lo(m, s % 2)
                    one_hots(it, 2 * s)
                    one_hots(it, 2 * s + 1)
            with dve.Fori(0, U_REST // 2 - 1) as mp:
                for k in range(2):
                    m = mp * 2 + (U_ROUTE + U_DENSE + k)
                    turn(m + 1, (k + 1) % 2)
                    u_lo(m, k)
            turn(P - 1, 1)
            u_lo(P - 2, 0)
            u_lo(P - 1, 1)

            for k in range(2):
                dve.wait_ge(a_store[k], 16 * 64)
                dve.wait_ge(g_store[k], 16 * 12)
            V.memset(zero[:, :], 0.0).then_inc(z_done, 1)
            dve.sem_inc(w_mult, 8)
            for dh in range(2):
                with dve.Fori(0, 8) as it:
                    for s in range(8):
                        slot = s % 2
                        dve.wait_ge(a_in[slot], it * 64 + 16 * (dh * 32 + s // 2 + 1))
                        dve.wait_ge(gg_in[s // 4], it * 16 + 16 * (dh * 8 + 1))
                        V.tensor_tensor(wt[:, slot, :, :].rearrange("p q (b t) -> p q b t", t=TB),
                                        at_[:, slot, :, :].rearrange("p q (b t) -> p q b t", t=TB),
                                        gt[:, s // 4, :, :].rearrange("p b (q t) -> p q b t", q=8)[:, 2 * (s % 4):2 * (s % 4) + 2, :, :],
                                        ALU.mult).then_inc(w_mult, 1)
                        split_lo(it * 8 + (BASE_V + dh * 64 + s), slot)
                        dve.wait_ge(wh_done, it * 8 + (dh * 64 + s + 1))
                        V.tensor_tensor(xTl[:, 2 * slot:2 * slot + 2, :], wt[:, slot, :, :],
                                        xTh[:, 2 * slot:2 * slot + 2, :].bitcast(F32), ALU.subtract).then_inc(wl_done, 1)
                dve.wait_ge(acc_done, dh + 1)
                for t in range(NT):
                    for c in range(2):
                        ysl = hh[:, t, dh * 1024 + c * W:dh * 1024 + (c + 1) * W]
                        V.tensor_tensor(ysl, bank[2 * t + c][:, :], ysl, ALU.add).then_inc(y_done, 1)

        @block.tensor
        def _(pe):
            MM, TR = nc.tensor.matmul, nc.tensor.transpose
            for one in (p_WT, s_S, s_w):
                pe.sem_inc(one, 1)
            pe.sem_inc(split_used, 2)
            pe.sem_inc(s_o, 2)
            pe.sem_inc(g_mm, 2)
            pe.wait_ge(S_const, 16 * 9)

            def norm_part(p):
                for t in range(NT):
                    pe.wait_ge(xs_ready, p * 3 + t + 1)
                    for q in range(4):
                        n = p * 12 + t * 4 + q
                        if n >= 4:
                            pe.wait_ge(tr_free, n - 3)
                        for i in range(4):
                            k = 4 * q + i
                            last = TR(bank[3 + q][:, i * P:(i + 1) * P], xs[:, t % 2, k * P:(k + 1) * P], ident)
                        last.then_inc(tr_ready, 1)
                pe.wait_ge(tr_free, p * 12 + 12)

            def three(out, h1, l1, h2, l2, first, last):
                MM(out, h1, h2, start=first, stop=False)
                MM(out, h1, l2, start=False, stop=False)
                return MM(out, l1, h2, start=False, stop=last)

            def weight_step(n, slot, kq, xh, xl, free):
                pe.wait_ge(lo_done, n + 3)
                for t in range(NT):
                    if kq == 0:
                        pe.wait_ge(*free(t))
                    for k in range(KQ):
                        c = slice(k * W, (k + 1) * W)
                        ts = slice(t * P, (t + 1) * P)
                        last = three(bank[t][:, :], xh[:, kq * KQ + k, ts], xl[:, kq * KQ + k, ts],
                                     ringH[:, slot, c], ringL[:, slot, c], kq == 0 and k == 0, kq == 3 and k == KQ - 1)
                    if t == NT - 1:
                        last.then_inc(split_used, 1)
                    elif kq == 3:
                        last.then_inc(proj_ready, 1)

            norm_part(0)
            pe.sem_inc(proj_free, 3)
            with pe.Fori(0, NG) as g:
                for s in range(12):
                    weight_step(g * 12 + s, s % 2, s % 4, xTh, xTl, lambda t, s=s: (proj_free, g * 9 + (s // 4 * 3 + t + 1)))
                pe.wait_ge(qk_ready, g + 1)
                pe.wait_ge(o_lo, g * 4 + 1)
                for m, bk in ((0, 5), (1, 6)):
                    for h in range(HG):
                        last = TR(bank[bk][:, h * P:(h + 1) * P], qk[:, m, 2, h * P:(h + 1) * P], ident)
                    last.then_inc(sT, 1)

                def p_trans(h):
                    for m in range(2):
                        for t in range(2):
                            last = TR(bank[3][:, (2 * m + t) * P:(2 * m + t + 1) * P], qk[:, m, t, h * P:(h + 1) * P], ident)
                    last.then_inc(p_tr, 1)

                def p_scores(h):
                    pe.wait_ge(p_qkT, g * 4 + (h + 1))
                    for qt in range(2):
                        nk = P * (qt + 1)
                        for c in range(2):
                            r = slice(64 * c, 64 * c + 64)
                            last = MM(pS[qt][:, c, :], qkT[r, h % 2, qt * P:(qt + 1) * P],
                                      qkT[r, h % 2, 256:256 + nk], start=True, stop=True)
                    last.then_inc(p_S, 1)

                def p_post(m):
                    h, qt = divmod(m, 2)
                    pe.wait_ge(p_W, g * 8 + (m + 1))
                    if m == 0:
                        pe.wait_ge(sTe, g * 2 + 2)
                    for kt in range(qt + 1):
                        last = TR(bank[6][:, kt * P:(kt + 1) * P], Wp[:, kt * P:(kt + 1) * P], ident)
                    last.then_inc(p_WT, 1)
                    pe.wait_ge(p_WTe, g * 8 + (m + 1))
                    pe.wait_ge(p_oe, g * 8 + (m + 1))
                    for kt in range(qt + 1):
                        last = MM(bank[7][:, 0:P], WTp[:, kt, :], vs[:, kt, h * P:(h + 1) * P], start=kt == 0, stop=kt == qt)
                    last.then_inc(p_o, 1)

                p_trans(0)
                pe.wait_ge(sTe, g * 2 + 2)
                p_scores(0)
                for h in range(HG):
                    if h + 1 < HG:
                        p_trans(h + 1)
                    p_post(2 * h)
                    p_post(2 * h + 1)
                    if h + 1 < HG:
                        p_scores(h + 1)

                def s_trans(b):
                    pe.wait_ge(cache_in[b % 2], g * 128 + 32 * (b // 2 + 1))
                    pe.wait_ge(s_kTe, g * 8 + (b + 1))
                    for h in range(HG):
                        for c in range(2):
                            last = TR(bank[3 + h // 2][:, (h % 2) * 256 + c * P:(h % 2) * 256 + (c + 1) * P],
                                      kc[:, b % 2, c, h * P:(h + 1) * P], ident)
                    last.then_inc(s_kt, 1)

                def s_scores(b):
                    pe.wait_ge(s_kTe, g * 8 + (b + 2))
                    pe.wait_ge(s_q, g * 8 + (b + 1))
                    pe.wait_ge(s_exp, g * 8 + (b + 1))
                    for h in range(HG):
                        r = slice(32 * h, 32 * h + 32)
                        MM(bank[5][r, 0:256], qcur[:, h, :], kTc[:, b % 2, h, :], start=True, stop=True)
                        last = MM(bank[5][r, 256:384], qcur[:, h, :], kTn[:, h, :], start=True, stop=True)
                    last.then_inc(s_S, 1)

                s_trans(0)
                s_scores(0)
                for b in range(DEC_B):
                    if b + 1 < DEC_B:
                        s_trans(b + 1)
                    pe.wait_ge(s_M, g * 8 + (b + 1))
                    pe.wait_ge(s_we, g * 8 + (b + 1))
                    for c in range(3):
                        last = MM(bank[6][:, c * P:(c + 1) * P], Ps[:, c * P:(c + 1) * P], Ms[:, :], start=True, stop=True)
                    last.then_inc(s_w, 1)
                    if b + 1 < DEC_B:
                        s_scores(b + 1)
                    pe.wait_ge(s_we, g * 8 + (b + 2))
                    pe.wait_ge(s_oe, g * 8 + (b + 1))
                    for h in range(HG):
                        for c in range(3):
                            rhs = vc[:, b % 2, c, h * P:(h + 1) * P] if c < 2 else vs[:, 2, h * P:(h + 1) * P]
                            last = MM(bank[7][32 * h:32 * h + 32, 0:P], wTs[:, c, 32 * h:32 * h + 32], rhs, start=c == 0, stop=c == 2)
                    last.then_inc(s_o, 1)
                pe.wait_ge(o_n, g + 1)
                for i in range(4):
                    for j in range(4):
                        last = TR(bank[3 + i][:, j * P:(j + 1) * P], oall[:, 4 * i + j, :], ident)
                    last.then_inc(o_t, 1)

            for kq in range(4):
                weight_step(BASE_POOL + kq, kq % 2, kq, xTh, xTl, lambda t: (proj_free, 27 + t + 1))
            pe.wait_ge(o_lo, 13)
            pe.wait_ge(proj_free, 3 + 30)
            for gg in range(4):
                for t in range(NT):
                    last = TR(bank[3 + gg][:, t * P:(t + 1) * P], ptok[:, t, gg * P:(gg + 1) * P], ident)
                last.then_inc(pl_tr, 1)
            pe.wait_ge(pl_in, 32)
            nh = DEC_B * HIST
            for gg in range(4):
                last = TR(bank[7][:, gg * nh:(gg + 1) * nh], hist[0:nh, gg * P:(gg + 1) * P], cst[0:nh, C_ID:C_ID + nh])
            last.then_inc(pl_tr, 1)
            for gg in range(4):
                pe.wait_ge(pl_d, gg + 1)
                MM(bank[3 + gg][:, 0:T], wpl[:, gg, :], dT[:, gg, :], start=True, stop=True).then_inc(pl_mm, 1)
            pe.wait_ge(pl_lo, 4)

            for s in range(16):
                nb, kq = divmod(s, 4)
                weight_step(BASE_WOUT + s, s % 2, kq, mixTh, mixTl,
                            lambda t, nb=nb: (h_done, (nb - 1) * 3 + t + 1) if nb else (proj_free, 30 + t + 1))
            norm_part(1)

            pe.wait_ge(key_in, 16)
            for c in range(2):
                last = TR(bank[7][:, c * P:(c + 1) * P], keyr[:, c, :], ident)
            last.then_inc(key_tr, 1)
            pe.wait_ge(key_ev, 1)

            def key_scores(nb):
                pe.wait_ge(qT_ev, nb * 4 + 4)
                if nb:
                    pe.wait_ge(sc_ev, nb * 3)
                for t in range(NT):
                    for sub in range(4):
                        last = MM(bank[4 + t][:, sub * P:(sub + 1) * P], qTk[:, sub, t * P:(t + 1) * P], keyT[:, sub % 2, :],
                                  start=True, stop=True)
                    last.then_inc(sc_rdy, 1)

            pe.wait_ge(h_done, 12)
            for nb in range(4):
                for kq in range(4):
                    n = BASE_WPQ + nb * 4 + kq
                    pe.wait_ge(lo_done, n + 3)
                    for sub in range(4):
                        if kq == 0 and nb:
                            pe.wait_ge(qT_ev, (nb - 1) * 4 + sub + 1)
                        for k in range(KQ):
                            c = slice(k * W + sub * P, k * W + (sub + 1) * P)
                            last = three(bank[sub][:, 0:T], ringH[:, kq % 2, c], ringL[:, kq % 2, c],
                                         xTh[:, kq * KQ + k, :], xTl[:, kq * KQ + k, :], kq == 0 and k == 0, kq == 3 and k == KQ - 1)
                        if sub == 3:
                            last.then_inc(split_used, 1)
                        elif kq == 3:
                            last.then_inc(qT_rdy, 1)
                    if kq == 0 and nb:
                        key_scores(nb - 1)
            key_scores(3)

            def u_step(m, k):
                pe.wait_ge(lo_done, m + (BASE_U + 3))
                pe.wait_ge(gelu_done, m + 1)
                for b in range(KC):
                    c = slice(b * P, (b + 1) * P)
                    last = three(bank[k][:, 0:T], ringH[:, k, c], ringL[:, k, c], xTh[:, b, :], xTl[:, b, :], b == 0, b == KC - 1)
                last.then_inc(split_used, 1)

            def dense_weights(it, qd):
                pe.wait_ge(ab_ready, it * 8 + (qd + 1))
                pe.wait_ge(g_ev, it * 8 + (qd + 1))
                for i in range(4):
                    last = MM(bank[6 + qd % 2][:, i * P:(i + 1) * P], onesA[:, qd % 2, i, :], onesB[:, qd % 2, i, :],
                              start=True, stop=True)
                last.then_inc(g_mm, 1)

            with pe.Fori(0, U_ROUTE // 2) as mp:
                for k in range(2):
                    u_step(mp * 2 + k, k)
            pe.wait_ge(rt_ready, 3)
            pe.wait_ge(sc_ev, 12)
            for i in range(3):
                for t in range(NT):
                    last = TR(bank[4 + i][:, t * P:(t + 1) * P], route[:, t, i, :], ident)
                last.then_inc(rt_tr, 1)
            pe.wait_ge(rt_ev, 2)
            with pe.Fori(0, NTB // 2) as it:
                for s in range(4):
                    u_step(it * 4 + (U_ROUTE + s), s % 2)
                    for qd in range(2 * s, 2 * s + 2):
                        dense_weights(it, qd)
            with pe.Fori(0, U_REST // 2) as mp:
                for k in range(2):
                    u_step(mp * 2 + (U_ROUTE + U_DENSE + k), k)

            pe.wait_ge(z_done, 2)
            pe.wait_ge(gelu_done, P + 2)
            for dh in range(2):
                if dh:
                    pe.wait_ge(y_done, 6)
                for i in range(6):
                    MM(bank[i][:, :], zero[:, 0:P], zero[:, :], start=True, stop=False)
                with pe.Fori(0, 8) as it:
                    for s in range(8):
                        slot = s % 2
                        pe.wait_ge(lo_done, it * 8 + (BASE_V + dh * 64 + s + 3))
                        pe.wait_ge(wl_done, it * 8 + (dh * 64 + s + 1))
                        for q in range(2):
                            for t in range(NT):
                                for c in range(2):
                                    cs = slice(q * 1024 + c * W, q * 1024 + (c + 1) * W)
                                    last = three(bank[2 * t + c][:, :], xTh[:, 2 * slot + q, t * P:(t + 1) * P],
                                                 xTl[:, 2 * slot + q, t * P:(t + 1) * P], ringH[:, slot, cs], ringL[:, slot, cs],
                                                 False, False)
                        last.then_inc(split_used, 1)
                for i in range(6):
                    last = MM(bank[i][:, :], zero[:, 0:P], zero[:, :], start=False, stop=True)
                last.then_inc(acc_done, 1)


INS = ["x_prompt", "x_sample", "cache_k", "cache_v", "state_pool", "norm1_g", "w_in", "w_pool", "pool_scale", "q_norm_g",
       "k_norm_g", "lambda_q1", "lambda_k1", "lambda_q2", "lambda_k2", "subln_g", "w_out", "norm2_g", "w_pq", "sub_keys",
       "u_tab", "v_tab"]
OUTS = [("y_prompt", (1, SEQ, D)), ("y_sample", (DEC_B, DEC_S, D)), ("k_prompt", (1, 1, SEQ, HEADS, 2, HD)),
        ("v_prompt", (1, 1, SEQ, HEADS, VD)), ("pool_prompt", (1, 1, HIST, DPOOL)),
        ("k_sample", (1, DEC_B, DEC_S, HEADS, 2, HD)), ("v_sample", (1, DEC_B, DEC_S, HEADS, VD)),
        ("pool_sample", (1, DEC_B, HIST, DPOOL))]


def kernel(**inputs):
    import numpy as _np
    import concourse.bacc as _bacc
    from concourse import mybir as _mybir
    from concourse.bass_utils import run_bass_kernel_spmd as _run

    nc = _bacc.Bacc("TRN2", target_bir_lowering=False, num_devices=1)
    arrays, ins, outs = {"in_cst": constants()}, {}, {}
    for name in INS:
        arrays["in_" + name] = _np.ascontiguousarray(inputs[name])
    for name, a in arrays.items():
        ins[name[3:]] = nc.dram_tensor(name, a.shape, _mybir.dt.from_np(a.dtype), kind="ExternalInput").ap()
    for name, shape in OUTS:
        outs[name] = nc.dram_tensor("out_" + name, shape, _mybir.dt.float32, kind="ExternalOutput").ap()
    hybrid_layer(nc, ins, outs)
    r = _run(nc, [arrays], core_ids=[0])
    return tuple(r.results[0]["out_" + name] for name, _ in OUTS)
```

```python
import math
from contextlib import ExitStack

import numpy as np

import concourse.bass as bass
from concourse import mybir

P = 128
D = 2048
KC = D // P
SEQ, DEC_B, DEC_S, PAST = 256, 8, 16, 256
NT = (SEQ + DEC_B * DEC_S) // P
T = NT * P
DPOOL, DATT, HEADS, HD, VD = 512, 1536, 12, 64, 128
NG = 3
HG = HEADS // NG
GW = HG * VD
HIST = 15
PH, TOPK, NKEY = 8, 16, 128
EPS = 1e-6
LAM_INIT = 0.8 - 0.6 * math.exp(-0.3)
QS = HD ** -0.5
NEG = -3.0e38
W = 512
KQ = 4
TB = 16
NTB = T // TB
N_WIN, N_WOUT, N_WPQ = 40, 16, 16
BASE_POOL = 36
BASE_WOUT = N_WIN
BASE_WPQ = BASE_WOUT + N_WOUT
BASE_U = BASE_WPQ + N_WPQ
BASE_V = BASE_U + P
N_PARTS = 18
U_ROUTE = NT * N_PARTS
U_DENSE = 4 * (NTB // 2)
U_REST = P - U_ROUTE - U_DENSE

AHEAD = 3

W_OUT_ORDER = (1, 2, 3, 0)

C_ID, C_IOTA, C_ROPE, C_PM, C_SM, C_SEL, C_CV, C_INV = 0, 128, 256, 304, 368, 608, 736, 738
C_END = C_INV + 64 + 6


def constants():
    c = np.zeros((P, C_END), np.float32)
    c[:, C_ID:C_ID + P] = np.eye(P, dtype=np.float32)
    c[:, C_IOTA:C_IOTA + P] = np.arange(P, dtype=np.float32)
    inv = np.float32(500000.0) ** (-np.arange(0, 16, 2, dtype=np.float32) / np.float32(16))
    pos = np.concatenate([np.arange(SEQ), PAST + np.arange(P) % DEC_S]).astype(np.float32)
    ang = (pos[:, None] * inv[None, :].astype(np.float32)).astype(np.float32)
    rope = np.stack([np.cos(ang), np.sin(ang)], 1).astype(np.float32)
    c[:, C_ROPE:C_PM] = rope.reshape(NT, P, 16).transpose(1, 0, 2).reshape(P, 48)
    c[0:64, C_PM:C_SM] = NEG
    c[:, C_SM:C_SEL] = NEG
    c[:, C_SM + 112:C_SM + 128] = 0.0
    for h in range(HG):
        for m in range(2):
            for q in range(DEC_S):
                c[32 * h + 16 * m + q, C_SEL + 32 * h + q] = 1.0
            c[32 * h + 16 * m:32 * h + 16 * m + 16, C_CV + m] = 1.0
    for g in range(4):
        w = 2 ** (g + 1)
        c[:, C_INV + 16 * g:C_INV + 16 * g + 16] = 1.0 / np.minimum(np.arange(16) + 1, w)
    return c


def hybrid_layer(nc, I, O):
    F32, F32R, U32 = mybir.dt.float32, mybir.dt.float32r, mybir.dt.uint32
    ALU, ACT, AX = mybir.AluOpType, mybir.ActivationFunctionType, mybir.AxisListType
    ds = bass.ds
    ctx = ExitStack()
    with ctx:
        ctx.enter_context(nc.allow_non_contiguous_dma(reason="small vectors"))
        KB = 1024
        base = (nc.sbuf_base + 63) // 64 * 64
        arena = ctx.enter_context(nc.sbuf_tensor("arena", [P, 207 * 256], F32, align_bytes=64))

        def at(name, kb, shape, dt=F32):
            return nc.alloc_sbuf_tensor_at(name, shape, dt, offset=base + int(kb * KB))

        xTh = at("xT_hi", 0, [P, KC, T], F32R)
        xTl = at("xT_lo", 24, [P, KC, T], F32R)
        ringH = at("ring_hi", 48, [P, 2, D], F32R)
        ringL = at("ring_lo", 64, [P, 2, D], F32R)
        raw = at("raw", 80, [P, 2, D])
        cst = at("cst", 96, [P, C_END])
        m0 = 96 + (C_END * 4) / KB
        prm = at("prm", m0, [P, 512])
        MX, WK = 101.5, 149.5
        mixTh = at("mixT_hi", MX, [P, KC, T], F32R)
        mixTl = at("mixT_lo", MX + 24, [P, KC, T], F32R)
        gqk = prm[:, 0:128].rearrange("p (c d) -> p c d", c=2)
        pscale = prm[:, 128:132]
        subg = prm[:, 132:133]
        lamv = prm[:, 133:134]
        cvec = prm[:, 134:135]
        cvt = prm[:, 135:136]
        lame = prm[:, 136:138]
        ssx = prm[:, 140:143]
        rtx = prm[:, 144:147]
        rrx = prm[:, 148:151]
        ss48 = prm[:, 152:200]
        rt48 = prm[:, 200:248]
        rr48 = prm[:, 248:296]
        so16 = prm[:, 296:312]
        ro16 = prm[:, 312:328]
        rn16 = prm[:, 328:344]
        pst = prm[:, 344:364].rearrange("p (s c) -> p s c", s=2)
        sst = prm[:, 364:370]
        lamin = prm[:, 370:374]
        epsv = prm[:, 374:375]
        nwt = prm[:, 376:424]
        lin = at("lambda_in", MX + 6, [P, 384])
        xin = at("x_tiles", WK, [P, NT, D])
        gbc = at("norm_gain", WK + 24, [P, D])
        junk = at("squares", WK + 32, [P, D])
        xs = at("x_normed", WK + 40, [P, 2, D])
        qk = at("qk", WK, [P, 2, NT, GW])
        vs = at("v_new", WK + 12, [P, NT, GW])
        kc = at("k_cache", WK + 18, [P, 2, 2, GW])
        vc = at("v_cache", WK + 26, [P, 2, 2, GW])
        oall = at("o_all", WK + 34, [P, 16, P])
        sq = at("qk_squares", WK + 42, [P, 6 * GW])
        kTc = at("kT_cache", WK + 42, [P, 2, HG, PAST])
        pP = at("p_prompt", MX, [P, 2, 2, 256])
        Wp = at("w_prompt", MX + 4, [P, 256])
        WTp = at("wT_prompt", MX + 5, [P, 2, P])
        qkT = at("qkT_prompt", MX + 24, [P, 2, 512])
        Ps = at("p_sample", WK + 50, [P, 384])
        Ms = at("combine", WK + 51.5, [P, P])
        wTs = at("wT_sample", WK + 52, [P, 3, P])
        qcur = at("q_blockdiag", WK + 53.5, [P, HG, 32])
        qTs = at("qT_sample", WK + 54, [P, HG, P])
        kTn = at("kT_new", WK + 56, [P, HG, P])
        UP = 528
        ub = at("pool_in", 6, [P, 4, UP])
        sA = at("pool_a", 24, [P, 4, UP])
        sB = at("pool_b", 32.25, [P, 4, UP])
        dT = at("pool_d", 14.25, [P, 4, T])
        ptok = at("pool_tok", 0, [P, NT, W])
        hist = at("pool_hist", WK + 42, [P, W])
        wpl = at("w_pool", WK + 44, [P, 4, P])
        hh = at("h", WK, [P, NT, D])
        scores = at("scores", MX, [P, NT, D])
        qTk = at("qT_keys", MX + 24, [P, 4, T])
        keyT = at("keysT", MX + 30, [P, 2, P])
        keyr = at("keys_raw", MX + 31, [P, 2, P])
        rT = at("route_T", WK + 48, [P, 3, T])
        onesA = at("onehot_a", WK + 40, [P, 2, 4, P])
        onesB = at("onehot_b", WK + 44, [P, 2, 4, P])
        sc = at("scores_cur", WK + 24, [P, 16, P])
        cand = at("cand", WK + 32, [P, PH, 256])
        eqb = at("eq", WK + 40, [P, PH, TOPK, TOPK])
        tv = at("top_values", WK + 48, [P, 16, 16])
        ti = at("top_index", WK + 49, [P, 16, 16], U32)
        tf = at("top_index_f", WK + 50, [P, 16, 16])
        bv = at("best", WK + 51, [P, PH, 16])
        bi = at("best_index", WK + 51.5, [P, PH, 16], U32)
        bhl = at("best_hl", WK + 52, [P, 2, PH, 16], U32)
        bhf = at("best_hl_f", WK + 53, [P, 2, PH, 16])
        route = at("route", MX + 43, [P, NT, 3, PH * TOPK])
        bst = at("route_stats", WK + 54, [P, 2, PH])
        gsb = at("g_block", WK + 24, [P, 2, P, TB])
        uT = at("u_turned", MX + 24, [P, 2, D])
        aout = at("gelu_out", MX + 40, [P, 2, T])
        zero = at("zeros", WK + 55.5, [P, W])
        gt = at("g_tile", MX, [P, 2, NTB, 8 * TB])
        at_ = at("a_tile", MX + 24, [P, 2, 2, T])
        wt = at("w_tile", MX + 30, [P, 2, 2, T])

        psum = ctx.enter_context(nc.psum_tensor("banks", [P, 8, 512], F32))
        bank = [psum[:, i, :] for i in range(8)]
        pS = [psum[:, 1:3, 0:P], psum[:, 1:3, P:3 * P]]
        Gd = nc.dram_tensor("g_dense", (NTB, P, P * TB), F32, kind="Internal").ap()
        Ad = nc.dram_tensor("a_dense", (P, P, T), F32, kind="Internal").ap()

        names = {}

        def sem(n):
            names[n] = ctx.enter_context(nc.semaphore(n))
            return names[n]

        S_const, small_in = sem("s_const"), sem("small_in")
        x_in = [sem(f"x_in{i}") for i in range(NT)]
        g_in1, g_in2 = sem("gain1_in"), sem("gain2_in")
        raw_ready = [sem("raw_ready0"), sem("raw_ready1")]
        hi_done, lo_done, split_used = sem("hi_done"), sem("lo_done"), sem("split_used")
        n_rt, xs_ready, tr_ready, tr_hi, tr_free = (sem(x) for x in ("n_rt", "xs_ready", "tr_ready", "tr_hi", "tr_free"))
        n_sq = sem("n_sq")
        lam_a, lam_b, lam_c = sem("lam_sums"), sem("lam_exp"), sem("lam_ready")
        proj_ready, proj_free = sem("proj_ready"), sem("proj_free")
        q_sq, q_ss, q_rt, qk_ready = sem("q_sq"), sem("q_ss"), sem("q_rt"), sem("qk_ready")
        kv_stored = sem("kv_stored")
        sT, sTe = sem("s_T"), sem("s_Te")
        p_tr, p_qkT, p_S, p_mx, p_exp, p_W, p_WT, p_WTe, p_o, p_oe = (sem("p_" + x) for x in "tr qkT S mx exp W WT WTe o oe".split())
        kc_in = [sem("k_cache_in0"), sem("k_cache_in1")]
        vc_in = [sem("v_cache_in0"), sem("v_cache_in1")]
        s_q, s_kt, s_kTe, s_S, s_mx, s_exp, s_M, s_w, s_we, s_o, s_oe = (sem("s_" + x) for x in "q kt kTe S mx exp M w we o oe".split())
        o_sq, o_ss, o_rt, o_n, o_t, o_hi, o_lo = (sem("o_" + x) for x in "sq ss rt n t hi lo".split())
        pl_in, pl_zero, pl_tr, pl_up, pl_d, pl_mm, pl_hi, pl_lo = (sem("pl_" + x) for x in "in zero tr up d mm hi lo".split())
        pool_out = sem("pool_out")
        h_in, h_done = sem("h_in"), sem("h_done")
        key_in, key_tr, key_ev, qT_rdy, qT_ev, sc_rdy, sc_ev = (sem(x) for x in "key_in key_tr key_ev qT_rdy qT_ev sc_rdy sc_ev".split())
        cur_ready, cur_free, best_rdy, best_exp, rt_ready, rt_tr, rt_ev = (sem(x) for x in "cur_ready cur_free best_rdy best_exp rt_ready rt_tr rt_ev".split())
        ab_ready, g_mm, g_ev = sem("ab_ready"), sem("g_mm"), sem("g_ev")
        g_store = [sem("g_store0"), sem("g_store1")]
        u_turn, gelu_done = sem("u_turn"), sem("gelu_done")
        a_store = [sem("a_store0"), sem("a_store1")]
        a_in = [sem("a_in0"), sem("a_in1")]
        gg_in = [sem("gt_in0"), sem("gt_in1")]
        w_mult, wh_done, wl_done, z_done, acc_done, y_done = (sem(x) for x in "w_mult wh_done wl_done z_done acc_done y_done".split())
        y_out = sem("y_out")
        g_free, a_free = sem("g_free"), sem("a_free")
        pool_passed, dve_passed = sem("pool_passed"), sem("dve_passed")

        ident = cst[:, C_ID:C_ID + P]
        iota = cst[:, C_IOTA:C_IOTA + P]

        u_v = I["u_tab"][0].rearrange("(r i q) (a d) -> a i q r d", r=4, i=32, q=P, a=4)
        v_v = I["v_tab"][0].rearrange("(p q) d -> p q d", q=P)

        def wait_block(eng, t, blk, n_last):
            if t < NT - 1:
                eng.wait_ge(proj_ready, blk * 2 + (t + 1))
            else:
                eng.wait_ge(split_used, n_last + 3)

        block = ctx.enter_context(nc.Block())

        @block.sync
        def _(sp):
            def load(n, slot, parts, free):
                sp.wait_ge(free[0], free[1])
                for dst, src in parts:
                    sp.dma_start(dst, src).then_inc(raw_ready[slot], 16)

            def weight_step(n, slot, w, kq, cols):
                load(n, slot, [(raw[:, slot, k * W:(k + 1) * W], w[(kq * KQ + k) * P:(kq * KQ + k + 1) * P, cols])
                               for k in range(KQ)], (lo_done, n + 1))

            with sp.Fori(0, NG) as g:
                for s in range(12):
                    blk, kq = divmod(s, 4)
                    weight_step(g * 12 + s, s % 2, I["w_in"][0], kq, ds(g * GW + DPOOL + blk * DATT, W))
            for kq in range(4):
                weight_step(BASE_POOL + kq, kq % 2, I["w_in"][0], kq, ds(0, W))
            for nb in range(4):
                for i, kq in enumerate(W_OUT_ORDER):
                    weight_step(nb * 4 + (BASE_WOUT + i), i % 2, I["w_out"][0], kq, slice(nb * W, (nb + 1) * W))
            pq = I["w_pq"][0].rearrange("(a b j) n -> a j b n", a=4, b=KC)
            with sp.Fori(0, 4) as nb:
                for kq in range(4):
                    n = nb * 4 + (BASE_WPQ + kq)
                    load(n, kq % 2, [(raw[32 * a:32 * a + 32, kq % 2, :].rearrange("p (b n) -> p b n", b=KQ),
                                      pq[a, :, kq * KQ:(kq + 1) * KQ, ds(nb * W, W)]) for a in range(4)], (lo_done, n + 1))
            with sp.Fori(0, P // 2) as mp:
                for k in range(2):
                    m = mp * 2 + k
                    load(m, k, [(raw[32 * a:32 * a + 32, k, :].rearrange("p (q r d) -> p q r d", r=4, q=1),
                                 u_v[a, :, ds(m, 1), :, :]) for a in range(4)], (u_turn, m + 1))
            sp.wait_ge(a_store[0], 16 * 64)
            sp.wait_ge(a_store[1], 16 * 64)
            sp.wait_ge(g_store[0], 16 * 12)
            sp.wait_ge(g_store[1], 16 * 12)
            for dh in range(2):
                with sp.Fori(0, 8) as it:
                    for s in range(8):
                        v = it * 8 + (dh * 64 + s)
                        n = it * 8 + (dh * 64 + s + BASE_V)
                        slot = s % 2
                        if s % 4 == 0:
                            sp.wait_ge(w_mult, it * 8 + (dh * 64 + s + 4))
                            q16 = it * 2 + s // 4
                            sp.dma_start(gt[:, s // 4, :, :],
                                         Gd.rearrange("b p x -> p b x")[:, :, ds(q16 * P, P)]).then_inc(gg_in[s // 4], 16)
                        sp.wait_ge(w_mult, it * 8 + (dh * 64 + s + 7))
                        i2 = it * 16 + 2 * s
                        sp.dma_start(at_[:, slot, :, :], Ad[ds(i2, 2), :, :].rearrange("q p t -> p q t")).then_inc(a_in[slot], 16)
                        load(n, slot, [(raw[32 * a:32 * a + 32, slot, :].rearrange("p (q d) -> p q d", q=2),
                                        v_v[32 * a:32 * a + 32, ds(i2, 2), dh * 1024:(dh + 1) * 1024]) for a in range(4)],
                             (lo_done, n + 1))
            sp.wait_ge(y_done, 12)
            for t in range(2):
                sp.dma_start(O["y_prompt"][0, t * P:(t + 1) * P, :], hh[:, t, :]).then_inc(y_out, 16)
            sp.dma_start(O["y_sample"].rearrange("b s d -> (b s) d"), hh[:, 2, :]).then_inc(y_out, 16)
            sp.wait_ge(y_out, 48)
            sp.wait_ge(kv_stored, NG * 96)
            sp.wait_ge(pool_out, 16 * 9)

        @block.gpsimd
        def _(pool):
            pool.sem_inc(g_free, 2)
            pool.sem_inc(a_free, 2)
            for m, nme in enumerate(("q_norm_g", "k_norm_g")):
                pool.dma_start(gqk[:, m, :], I[nme].broadcast_to([P, HD])).then_inc(small_in, 16)
            pool.dma_start(pscale, I["pool_scale"][0].rearrange("(g c) -> c g", c=P)).then_inc(small_in, 16)
            pool.dma_start(subg, I["subln_g"].rearrange("o c -> c o")).then_inc(small_in, 16)
            for m, nme in enumerate(("lambda_q1", "lambda_k1", "lambda_q2", "lambda_k2")):
                pool.dma_start(lin[:, m * HD:(m + 1) * HD], I[nme].broadcast_to([P, HD])).then_inc(small_in, 16)

            def loop_wait(sem, value, signal=pool_passed):
                pool.wait_ge(sem, value)
                pool.sem_inc(signal, 1)

            pool.wait_ge(tr_free, 12)
            with pool.Fori(0, NG) as g:
                for b in range(DEC_B):
                    j = b % 2
                    loop_wait(s_kt, g * 8 + (b + 1))
                    kv = I["cache_k"][0, b].rearrange("(c p) h m e -> p c (h m e)", p=P)
                    pool.dma_start(kc[:, j, :, :], kv[:, :, ds(g * GW, GW)]).then_inc(kc_in[j], 16)
                    loop_wait(s_o, g * 8 + (b + 1))
                    vv = I["cache_v"][0, b].rearrange("(c p) h e -> p c (h e)", p=P)
                    pool.dma_start(vc[:, j, :, :], vv[:, :, ds(g * GW, GW)]).then_inc(vc_in[j], 16)
                    if b == 1:
                        loop_wait(qk_ready, g * 2 + 2)
                        loop_wait(proj_free, g * 9 + (3 + 9))
                        kp = O["k_prompt"][0, 0].rearrange("s h m e -> s (h m e)")
                        vp = O["v_prompt"][0, 0].rearrange("s h e -> s (h e)")
                        ks = O["k_sample"][0].rearrange("b s h m e -> (b s) (h m e)")
                        vv = O["v_sample"][0].rearrange("b s h e -> (b s) (h e)")
                        for t in range(2):
                            pool.dma_start(kp[t * P:(t + 1) * P, ds(g * GW, GW)], qk[:, 1, t, :]).then_inc(kv_stored, 16)
                            pool.dma_start(vp[t * P:(t + 1) * P, ds(g * GW, GW)], vs[:, t, :]).then_inc(kv_stored, 16)
                        pool.dma_start(ks[:, ds(g * GW, GW)], qk[:, 1, 2, :]).then_inc(kv_stored, 16)
                        pool.dma_start(vv[:, ds(g * GW, GW)], vs[:, 2, :]).then_inc(kv_stored, 16)
            pool.wait_ge(proj_free, 3 + 30)
            pool.dma_start(O["pool_prompt"][0, 0], ptok[P - HIST:P, 1, :]).then_inc(pool_out, 16)
            for b in range(DEC_B):
                pool.dma_start(O["pool_sample"][0, b], ptok[16 * b + 1:16 * b + 16, 2, :]).then_inc(pool_out, 16)
            def store_gelu(m, k):
                loop_wait(gelu_done, m + 3)
                pool.dma_start(Ad[ds(m, 1), :, :].rearrange("o p x -> (o p) x"), aout[:, k, :]).then_inc(a_store[k], 16)

            def stored_gelu(mp):
                for k in range(2):
                    loop_wait(a_store[k], mp * 16 + 16, a_free)

            with pool.Fori(0, U_ROUTE // 2) as mp:
                for k in range(2):
                    store_gelu(mp * 2 + k, k)
                stored_gelu(mp)
            with pool.Fori(0, NTB // 2) as it:
                for sl in range(2):
                    for k in range(2):
                        store_gelu(it * 4 + (U_ROUTE + 2 * sl + k), k)
                    stored_gelu(it * 2 + (U_ROUTE // 2 + sl))
                    loop_wait(g_ev, it * 8 + (4 * sl + 4 + 2))
                    pool.dma_start(Gd[ds(it * 2 + sl, 1), :, :].rearrange("o p x -> (o p) x"),
                                   gsb[:, sl, :, :].rearrange("p a b -> p (a b)")).then_inc(g_store[sl], 16)
                    loop_wait(g_store[sl], it * 16 + 16, g_free)
            with pool.Fori(0, U_REST // 2) as mp:
                for k in range(2):
                    store_gelu(mp * 2 + (U_ROUTE + U_DENSE + k), k)
                stored_gelu(mp + (U_ROUTE + U_DENSE) // 2)

        @block.scalar
        def _(act):
            A = nc.scalar.activation
            for one in (p_oe, s_kTe, s_exp, s_we, s_oe, rt_ev):
                act.sem_inc(one, 1)
            act.sem_inc(gelu_done, 2)
            act.sem_inc(g_ev, 2)
            xp = [I["x_prompt"][0, 0:P, :], I["x_prompt"][0, P:2 * P, :], I["x_sample"].rearrange("b s d -> (b s) d")]
            act.dma_start(xin[:, 0, :], xp[0]).then_inc(x_in[0], 16)
            act.dma_start(cst[:, :], I["cst"]).then_inc(S_const, 16)
            act.dma_start(gbc[:, :], I["norm1_g"].broadcast_to([P, D])).then_inc(g_in1, 16)
            for t in range(1, NT):
                act.dma_start(xin[:, t, :], xp[t]).then_inc(x_in[t], 16)

            def split_hi(n, slot, src=None):
                if src is None:
                    act.wait_ge(raw_ready[slot], n * 32 + (64 - 32 * (slot % 2)))
                act.wait_ge(split_used, n + 1)
                A(ringH[:, slot, :], raw[:, slot, :], ACT.Copy).then_inc(hi_done, 1)

            def norm_part(p, src, ready):
                def root(t):
                    act.wait_ge(*ready(t))
                    A(junk[:, :], src[:, t, :], ACT.Square, accum_out=ssx[:, t:t + 1]).then_inc(n_sq, 1)
                    act.wait_ge(n_sq, p * 3 + t + 1)
                    A(rtx[:, t:t + 1], ssx[:, t:t + 1], ACT.Sqrt, scale=1.0 / D, bias=epsv).then_inc(n_rt, 1)

                def hi(t):
                    for q in range(4):
                        n = p * 12 + t * 4 + q
                        act.wait_ge(tr_ready, n + 1)
                        A(xTh[:, 4 * q:4 * q + 4, t * P:(t + 1) * P],
                          bank[3 + q][:, :].rearrange("p (k t) -> p k t", k=4), ACT.Copy).then_inc(tr_hi, 1)

                root(0)
                root(1)
                root(2)
                hi(0)
                hi(1)
                hi(2)

            act.wait_ge(S_const, 16)
            act.wait_ge(z_done, 1)
            norm_part(0, xin, lambda t: (x_in[t], 16))

            for s in range(AHEAD):
                split_hi(s, s % 2)
            act.wait_ge(small_in, 16 * 8)
            act.wait_ge(lam_a, 1)
            A(lame, lamin[:, 0:2], ACT.Exp).then_inc(lam_b, 1)
            with act.Fori(0, NG) as g:
                def evac_block(blk, tiles=range(NT)):
                    dst = qk[:, blk, :, :] if blk < 2 else vs[:, :, :]
                    for t in tiles:
                        wait_block(act, t, g * 3 + blk, g * 12 + (4 * blk + 3))
                        A(dst[:, t, :], bank[t][:, :], ACT.Copy).then_inc(proj_free, 1)

                for s in range(AHEAD, 12):
                    split_hi(g * 12 + s, s % 2)
                    m = s // 4 - 1
                    if s in (4, 8):
                        evac_block(m)
                        act.wait_ge(proj_free, g * 9 + (3 + 3 * m + 3))
                        A(sq[:, m * 3 * GW:(m + 1) * 3 * GW], qk[:, m, :, :].rearrange("p b c -> p (b c)"), ACT.Square).then_inc(q_sq, 1)
                    if s in (5, 9):
                        act.wait_ge(q_ss, g * 2 + (m + 1))
                        A(rt48[:, 24 * m:24 * m + 24], ss48[:, 24 * m:24 * m + 24], ACT.Sqrt, scale=1.0 / HD, bias=epsv).then_inc(q_rt, 1)
                def p_evac(h):
                    act.wait_ge(p_tr, g * 4 + (h + 1))
                    A(qkT[:, h % 2, :], bank[0][:, :], ACT.Copy).then_inc(p_qkT, 1)

                def p_exps(m):
                    qt = m % 2
                    nk = P * (qt + 1)
                    act.wait_ge(p_mx, g * 8 + (m // 2 * 2 + 2))
                    for c in range(2):
                        last = A(pP[:, qt, c, 0:nk], pS[qt][:, c, :], ACT.Exp,
                                 scale=QS, bias=pst[:, qt, 2 + c:3 + c], accum_out=pst[:, qt, 4 + c:5 + c])
                    last.then_inc(p_exp, 1)

                def p_wev(m):
                    nkt = m % 2 + 1
                    act.wait_ge(p_WT, g * 8 + (m + 2))
                    A(WTp[:, 0:nkt, :].rearrange("p a b -> p (a b)"), bank[3][:, 0:nkt * P], ACT.Copy).then_inc(p_WTe, 1)

                def p_oev(m):
                    act.wait_ge(p_o, g * 8 + (m + 1))
                    A(oall[:, m, :], bank[3][:, 0:P], ACT.Copy).then_inc(p_oe, 1)

                def s_kev(b):
                    act.wait_ge(s_kt, g * 8 + (b + 3))
                    for i in range(2):
                        last = A(kTc[:, b % 2, 2 * i:2 * i + 2, :].rearrange("p h k -> p (h k)"), bank[4 + i][:, :], ACT.Copy)
                    last.then_inc(s_kTe, 1)

                evac_block(2, (0, 1))
                act.wait_ge(qk_ready, g * 2 + 2)
                s_kev(0)
                act.wait_ge(sT, g * 2 + 2)
                A(qTs[:, :, :].rearrange("p h t -> p (h t)"), bank[6][:, :], ACT.Copy).then_inc(sTe, 1)
                A(kTn[:, :, :].rearrange("p h t -> p (h t)"), bank[7][:, :], ACT.Copy).then_inc(sTe, 1)
                evac_block(2, (2,))
                p_evac(0)
                p_exps(0)
                p_exps(1)
                for b in range(DEC_B):
                    act.wait_ge(s_mx, g * 8 + (b + 1))
                    act.wait_ge(s_w, g * 8 + (b + 1))
                    A(Ps[:, :], bank[6][:, 0:384], ACT.Exp, scale=QS, bias=sst[:, 1:2],
                      accum_out=sst[:, 2:3]).then_inc(s_exp, 1)
                    if b + 1 < DEC_B:
                        s_kev(b + 1)
                    p_wev(b)
                    if b % 2 == 0 and b + 2 < DEC_B:
                        p_evac(b // 2 + 1)
                    act.wait_ge(s_w, g * 8 + (b + 2))
                    A(wTs[:, :, :].rearrange("p a b -> p (a b)"), bank[7][:, 0:384], ACT.Copy).then_inc(s_we, 1)
                    p_oev(b)
                    if b % 2 == 1 and b + 1 < DEC_B:
                        p_exps(b + 1)
                        p_exps(b + 2)
                    if b in (0, 2):
                        split_hi(g * 12 + (12 + b // 2), b // 2)
                    if b == 7:
                        split_hi(g * 12 + 14, 0)
                    act.wait_ge(s_o, g * 8 + (b + 3))
                    A(oall[:, 8 + b, :], bank[7][:, 0:P], ACT.Copy).then_inc(s_oe, 1)
                act.wait_ge(s_oe, g * 8 + 9)
                act.wait_ge(p_oe, g * 8 + 9)
                A(sq[:, 0:D], oall[:, :, :].rearrange("p a b -> p (a b)"), ACT.Square).then_inc(o_sq, 1)
                act.wait_ge(o_ss, g + 1)
                A(ro16, so16, ACT.Sqrt, scale=1.0 / VD, bias=epsv).then_inc(o_rt, 1)
                for i in range(4):
                    act.wait_ge(o_t, g * 4 + (i + 1))
                    if i < 2:
                        A(mixTh[:, ds(g * 4 + (4 + 2 * i), 2), 0:SEQ], bank[3 + i][:, :].rearrange("p (h t) -> p h t", h=2),
                          ACT.Copy, scale=subg).then_inc(o_hi, 1)
                    else:
                        for b in range(4):
                            c0 = SEQ + 16 * (4 * (i - 2) + b)
                            last = A(mixTh[:, ds(g * 4 + 4, 4), c0:c0 + 16],
                                     bank[3 + i][:, b * P:(b + 1) * P].rearrange("p (h t) -> p h t", h=4)[:, :, 0:16],
                                     ACT.Copy, scale=subg)
                        last.then_inc(o_hi, 1)
                act.wait_ge(kv_stored, g * 96 + 96)

            for kq in range(AHEAD, 4):
                split_hi(BASE_POOL + kq, kq % 2)
            act.wait_ge(o_lo, 13)
            act.wait_ge(kv_stored, NG * 96)
            act.dma_start(hist[0:DEC_B * HIST, :], I["state_pool"][0].rearrange("b j c -> (b j) c")).then_inc(pl_in, 16)
            act.dma_start(wpl[:, :, :], I["w_pool"][0].rearrange("g c d -> c g d")).then_inc(pl_in, 16)
            for t in range(NT):
                wait_block(act, t, 9, BASE_POOL + 3)
                A(ptok[:, t, :], bank[t][:, :], ACT.Copy).then_inc(proj_free, 1)
            for t in range(NT):
                act.dma_start(hh[:, t, :], xp[t]).then_inc(h_in, 16)
            act.dma_start(gbc[:, :], I["norm2_g"].broadcast_to([P, D])).then_inc(g_in2, 16)
            split_hi(BASE_WOUT, 0)
            split_hi(BASE_WOUT + 1, 1)
            act.wait_ge(pl_zero, 1)
            for gg in range(4):
                act.wait_ge(pl_tr, gg + 1)
                A(ub[:, gg, 16:272], bank[3 + gg][:, 0:256], ACT.Copy)
                A(ub[:, gg, 272:528].rearrange("p (b s) -> p b s", b=8)[:, :, 16:32],
                  bank[3 + gg][:, 256:384].rearrange("p (b s) -> p b s", b=8), ACT.Copy).then_inc(pl_up, 1)
            act.wait_ge(pl_tr, 5)
            for gg in range(4):
                last = A(ub[:, gg, 272:528].rearrange("p (b s) -> p b s", b=8)[:, :, 1:16],
                         bank[7][:, gg * 120:(gg + 1) * 120].rearrange("p (b s) -> p b s", b=8), ACT.Copy)
            last.then_inc(pl_up, 1)
            split_hi(BASE_WOUT + 2, 0)
            split_hi(BASE_WOUT + 3, 1)
            for gg in range(4):
                act.wait_ge(pl_mm, gg + 1)
                A(mixTh[:, gg, :], bank[3 + gg][:, 0:T], ACT.Copy, scale=pscale[:, gg:gg + 1]).then_inc(pl_hi, 1)
            for s in range(4, 16):
                split_hi(BASE_WOUT + s, s % 2)
            act.wait_ge(pool_out, 16 * 9)
            norm_part(1, hh, lambda t: (h_done, 10 + t))
            act.dma_start(keyr[:, :, :], I["sub_keys"][0].rearrange("c k d -> k c d")).then_inc(key_in, 16)
            act.wait_ge(key_tr, 1)
            A(keyT[:, :, :].rearrange("p c k -> p (c k)"), bank[7][:, 0:256], ACT.Copy).then_inc(key_ev, 1)

            def score_evac(nb):
                for t in range(NT):
                    act.wait_ge(sc_rdy, nb * 3 + t + 1)
                    A(scores[:, t, nb * W:(nb + 1) * W], bank[4 + t][:, :], ACT.Copy).then_inc(sc_ev, 1)

            def q_evac(nb):
                for sub in range(4):
                    if sub < 3:
                        act.wait_ge(qT_rdy, nb * 3 + sub + 1)
                    else:
                        act.wait_ge(split_used, BASE_WPQ + nb * 4 + 3 + 3)
                    A(qTk[:, sub, :], bank[sub][:, 0:T], ACT.Copy).then_inc(qT_ev, 1)

            for s in range(16):
                split_hi(BASE_WPQ + s, s % 2)
                if s % 4 == 0 and s:
                    q_evac(s // 4 - 1)
                if s % 4 == 1 and s > 1:
                    score_evac(s // 4 - 1)
            q_evac(3)
            score_evac(3)

            act.wait_ge(sc_ev, 12)

            def u_hi(m, k):
                act.wait_ge(u_turn, m + 3)
                act.wait_ge(split_used, m + (BASE_U + 1))
                A(ringH[:, k, :].rearrange("p (b r i) -> p r b i", b=KC, r=4),
                  uT[:, k, :].rearrange("p (r b i) -> p r b i", r=4, b=KC), ACT.Copy).then_inc(hi_done, 1)

            def gelu(m, k):
                act.wait_ge(split_used, m + (BASE_U + 3))
                act.wait_ge(a_free, m + 1)
                A(aout[:, k, :], bank[k][:, 0:T], ACT.Gelu_apprx_tanh).then_inc(gelu_done, 1)

            u_hi(0, 0)
            with act.Fori(0, NT) as t:
                act.wait_ge(cur_free, t + 1)
                A(sc[:, :, :].rearrange("p a b -> p (a b)"), scores[:, ds(t, 1), :].rearrange("p o x -> p (o x)"), ACT.Copy).then_inc(cur_ready, 1)
                for j in range(N_PARTS):
                    m = t * N_PARTS + j
                    u_hi(m + 1, (j + 1) % 2)
                    gelu(m, j % 2)
                    if j == 13:
                        act.wait_ge(best_rdy, t + 1)
                        A(bv[:, :, :], bv[:, :, :], ACT.Exp).then_inc(best_exp, 1)
            act.wait_ge(rt_tr, 3)
            A(rT[:, :, :].rearrange("p a t -> p (a t)")[:, 0:2 * T].rearrange("p (c t) -> p c t", c=2),
              psum[:, 4:6, 0:T], ACT.Copy)
            A(rT[:, 2, :], bank[6][:, 0:T], ACT.Copy).then_inc(rt_ev, 1)
            with act.Fori(0, NTB // 2) as it:
                for s in range(4):
                    m = it * 4 + (U_ROUTE + s)
                    u_hi(m + 1, (s + 1) % 2)
                    gelu(m, s % 2)
                    sl = s // 2
                    if s % 2 == 0:
                        act.wait_ge(g_free, it * 2 + (sl + 1))
                    for qd in range(2 * s, 2 * s + 2):
                        act.wait_ge(g_mm, it * 8 + (qd + 3))
                        c0 = 4 * (qd % 4)
                        A(gsb[:, sl, :, c0:c0 + 4].rearrange("p i t -> p t i"),
                          bank[6 + qd % 2][:, :].rearrange("p (t i) -> p t i", t=4), ACT.Copy).then_inc(g_ev, 1)
            with act.Fori(0, U_REST // 2 - 1) as mp:
                for k in range(2):
                    m = mp * 2 + (U_ROUTE + U_DENSE + k)
                    u_hi(m + 1, (k + 1) % 2)
                    gelu(m, k)
            u_hi(P - 1, 1)
            gelu(P - 2, 0)
            gelu(P - 1, 1)

            for dh in range(2):
                with act.Fori(0, 8) as it:
                    for s in range(8):
                        split_hi_v = it * 8 + (BASE_V + dh * 64 + s)
                        split_hi(split_hi_v, s % 2)
                        act.wait_ge(w_mult, it * 8 + (dh * 64 + s + 9))
                        A(xTh[:, 2 * (s % 2):2 * (s % 2) + 2, :], wt[:, s % 2, :, :], ACT.Copy).then_inc(wh_done, 1)

        @block.vector
        def _(dve):
            V = nc.vector

            def drain():
                dve.drain()

            def refined_rsqrt(r, root, total, tmp, n):
                V.reciprocal(r, root)
                V.tensor_scalar(total, total, 1.0 / n, EPS, ALU.mult, ALU.add)
                drain()
                V.tensor_tensor(tmp, r, r, ALU.mult)
                drain()
                V.tensor_tensor(tmp, tmp, total, ALU.mult)
                drain()
                V.tensor_scalar(tmp, tmp, -0.5, 1.5, ALU.mult, ALU.add)
                drain()
                V.tensor_tensor(r, r, tmp, ALU.mult)
                drain()

            for one in (o_lo, cur_free):
                dve.sem_inc(one, 1)
            dve.sem_inc(lo_done, 2)
            V.memset(epsv, EPS).then_inc(z_done, 1)
            def split_lo(n, slot):
                dve.wait_ge(hi_done, n + 1)
                V.tensor_tensor(ringL[:, slot, :], raw[:, slot, :], ringH[:, slot, :].bitcast(F32), ALU.subtract).then_inc(lo_done, 1)

            def norm_part(p, src, gain, before=lambda t: None):
                def scaled(t):
                    dve.wait_ge(n_rt, p * 3 + t + 1)
                    refined_rsqrt(rrx[:, t:t + 1], rtx[:, t:t + 1], ssx[:, t:t + 1], nwt[:, 0:1], D)
                    if t == 0:
                        dve.wait_ge(*gain)
                    if t == 2:
                        dve.wait_ge(tr_ready, p * 12 + 4)
                    if p == 0:
                        V.scalar_tensor_tensor(out=xs[:, t % 2, :], in0=src[:, t, :], scalar=rrx[:, t:t + 1], in1=gbc[:, :],
                                               op0=ALU.mult, op1=ALU.mult).then_inc(xs_ready, 1)
                    else:
                        for a in range(4):
                            last = V.scalar_tensor_tensor(
                                out=xs[:, t % 2, :].rearrange("p (b a j) -> p a b j", b=KC, a=4)[:, a, :, :],
                                in0=src[:, t, a * 512:(a + 1) * 512].rearrange("p (b j) -> p b j", b=KC), scalar=rrx[:, t:t + 1],
                                in1=gbc[:, a * 512:(a + 1) * 512].rearrange("p (b j) -> p b j", b=KC),
                                op0=ALU.mult, op1=ALU.mult)
                        last.then_inc(xs_ready, 1)

                def lo(t):
                    for q in range(4):
                        n = p * 12 + t * 4 + q
                        dve.wait_ge(tr_hi, n + 1)
                        V.tensor_tensor(xTl[:, 4 * q:4 * q + 4, t * P:(t + 1) * P],
                                        bank[3 + q][:, :].rearrange("p (k t) -> p k t", k=4),
                                        xTh[:, 4 * q:4 * q + 4, t * P:(t + 1) * P].bitcast(F32), ALU.subtract).then_inc(tr_free, 1)

                before(0)
                scaled(0)
                before(1)
                before(2)
                scaled(1)
                lo(0)
                scaled(2)
                lo(1)
                lo(2)

            norm_part(0, xin, (g_in1, 16))
            dve.wait_ge(tr_free, 12)

            for s in range(AHEAD):
                split_lo(s, s % 2)
            dve.wait_ge(S_const, 16)
            dve.wait_ge(small_in, 16 * 8)
            lv = lin[:, 0:4 * HD].rearrange("p (m c e) -> p m c e", m=2, c=2)
            V.tensor_tensor(lin[:, 256:384].rearrange("p (m e) -> p m e", m=2), lv[:, :, 0, :], lv[:, :, 1, :], ALU.mult)
            drain()
            V.tensor_reduce(lamin[:, 0:2], lin[:, 256:384].rearrange("p (m e) -> p m e", m=2), AX.X, ALU.add).then_inc(lam_a, 1)
            dve.wait_ge(lam_b, 1)
            V.tensor_tensor(lamv, lame[:, 0:1], lame[:, 1:2], ALU.subtract)
            drain()
            V.tensor_scalar(lamv, lamv, LAM_INIT, None, ALU.add)
            drain()
            V.tensor_scalar(cvt, cst[:, C_CV + 1:C_CV + 2], lamv, None, ALU.mult)
            drain()
            V.tensor_tensor(cvec, cst[:, C_CV:C_CV + 1], cvt, ALU.subtract)
            drain()

            with dve.Fori(0, NG) as g:
                rope = cst[:, C_ROPE:C_PM].rearrange("p (t c e) -> p t c e", t=NT, c=2)
                tmp = sq[:, 0:4 * 192].rearrange("p (k t h e) -> p k t h e", k=4, t=NT, h=8)
                for s in range(AHEAD, 12):
                    split_lo(g * 12 + s, s % 2)
                    m = s // 4 - 1
                    c24 = slice(24 * m, 24 * m + 24)
                    if s in (5, 9):
                        dve.wait_ge(q_sq, g * 2 + (m + 1))
                        V.tensor_reduce(ss48[:, c24], sq[:, m * 3 * GW:(m + 1) * 3 * GW].rearrange("p (a e) -> p a e", e=HD),
                                        AX.X, ALU.add).then_inc(q_ss, 1)
                    elif s in (6, 10):
                        dve.wait_ge(q_rt, g * 2 + (m + 1))
                        refined_rsqrt(rr48[:, c24], rt48[:, c24], ss48[:, c24], nwt[:, 0:24], HD)
                        qm = qk[:, m, :, :].rearrange("p t (h e) -> p (t h) e", e=HD)
                        V.tensor_tensor(qm, qm, rr48[:, c24].unsqueeze(2).broadcast_to([P, 24, HD]), ALU.mult)
                        drain()
                        V.tensor_tensor(qm, qm, gqk[:, m:m + 1, :].broadcast_to([P, 24, HD]), ALU.mult)
                        drain()
                    elif s in (7, 11):
                        qh = qk[:, m, :, :].rearrange("p t (h e) -> p t h e", e=HD)
                        cos = rope[:, :, 0:1, :].broadcast_to([P, NT, 8, 8])
                        sin = rope[:, :, 1:2, :].broadcast_to([P, NT, 8, 8])
                        x1, x2 = qh[:, :, :, 0:8], qh[:, :, :, 8:16]
                        for k, (a, b) in enumerate(((x1, cos), (x2, sin), (x2, cos), (x1, sin))):
                            V.tensor_tensor(tmp[:, k], a, b, ALU.mult)
                        drain()
                        V.tensor_tensor(qh[:, :, :, 0:8], tmp[:, 0], tmp[:, 1], ALU.subtract)
                        V.tensor_tensor(qh[:, :, :, 8:16], tmp[:, 2], tmp[:, 3], ALU.add).then_inc(qk_ready, 1)

                pm = cst[:, C_PM:C_SM]

                def p_max(m):
                    qt = m % 2
                    nk = P * (qt + 1)
                    dve.wait_ge(p_S, g * 4 + (m // 2 + 1))
                    s2 = pS[qt]
                    V.tensor_tensor(s2[:, :, nk - 64:nk], s2[:, :, nk - 64:nk], pm.unsqueeze(1).broadcast_to([P, 2, 64]), ALU.add)
                    drain()
                    V.tensor_reduce(pst[:, qt, 0:2], s2[:, :, 0:nk], AX.X, ALU.max)
                    drain()
                    V.tensor_scalar(pst[:, qt, 2:4], pst[:, qt, 0:2], -QS, None, ALU.mult).then_inc(p_mx, 1)

                def p_comb(m):
                    qt = m % 2
                    nk = P * (qt + 1)
                    dve.wait_ge(p_exp, g * 8 + (m + 1))
                    V.reciprocal(pst[:, qt, 6:8], pst[:, qt, 4:6])
                    drain()
                    V.tensor_tensor(pst[:, qt, 8:9], pst[:, qt, 7:8], lamv, ALU.mult)
                    drain()
                    dve.wait_ge(p_WT, g * 8 + (m + 1))
                    V.tensor_scalar(Wp[:, 0:nk], pP[:, qt, 1, 0:nk], pst[:, qt, 8:9], None, ALU.mult)
                    drain()
                    V.scalar_tensor_tensor(out=Wp[:, 0:nk], in0=pP[:, qt, 0, 0:nk], scalar=pst[:, qt, 6:7], in1=Wp[:, 0:nk],
                                           op0=ALU.mult, op1=ALU.subtract).then_inc(p_W, 1)

                def q_diag(b):
                    dve.wait_ge(s_S, g * 8 + (b + 1))
                    V.tensor_copy(qcur[0:64, :, 0:16], qTs[0:64, :, 16 * b:16 * b + 16])
                    V.tensor_copy(qcur[64:128, :, 16:32], qTs[64:128, :, 16 * b:16 * b + 16]).then_inc(s_q, 1)

                def s_max(b):
                    dve.wait_ge(s_S, g * 8 + (b + 2))
                    V.tensor_tensor(bank[6][:, 256:384], bank[6][:, 256:384], cst[:, C_SM + 112 - 16 * b:C_SM + 240 - 16 * b], ALU.add)
                    drain()
                    V.tensor_reduce(sst[:, 0:1], bank[6][:, 0:384], AX.X, ALU.max)
                    drain()
                    V.tensor_scalar(sst[:, 1:2], sst[:, 0:1], -QS, None, ALU.mult).then_inc(s_mx, 1)

                V.memset(qcur[:, :, :], 0.0)
                drain()
                dve.wait_ge(sTe, g * 2 + 2)
                q_diag(0)
                p_max(0)
                p_max(1)
                for b in range(DEC_B):
                    s_max(b)
                    if b + 1 < DEC_B:
                        q_diag(b + 1)
                    p_comb(b)
                    dve.wait_ge(s_exp, g * 8 + (b + 2))
                    V.reciprocal(sst[:, 3:4], sst[:, 2:3])
                    drain()
                    V.tensor_scalar(Ms[:, :], cst[:, C_SEL:C_SEL + P], sst[:, 3:4], cvec, ALU.mult, ALU.mult).then_inc(s_M, 1)
                    if b % 2 == 1 and b + 1 < DEC_B:
                        p_max(b + 1)
                        p_max(b + 2)
                    if b in (2, 4):
                        split_lo(g * 12 + (12 + b // 2 - 1), b // 2 - 1)
                    if b == 7:
                        split_lo(g * 12 + 14, 0)
                dve.wait_ge(o_sq, g + 1)
                V.tensor_reduce(so16, sq[:, 0:D].rearrange("p (a e) -> p a e", e=VD), AX.X, ALU.add).then_inc(o_ss, 1)
                dve.wait_ge(o_rt, g + 1)
                refined_rsqrt(rn16, ro16, so16, nwt[:, 0:16], VD)
                V.tensor_scalar(rn16, rn16, 1.0 - LAM_INIT, None, ALU.mult)
                drain()
                V.tensor_tensor(oall[:, :, :], oall[:, :, :], rn16.unsqueeze(2).broadcast_to([P, 16, VD]), ALU.mult).then_inc(o_n, 1)
                for i in range(4):
                    dve.wait_ge(o_hi, g * 4 + (i + 1))
                    if i < 2:
                        mh = mixTh[:, ds(g * 4 + (4 + 2 * i), 2), 0:SEQ]
                        ml = mixTl[:, ds(g * 4 + (4 + 2 * i), 2), 0:SEQ]
                        V.scalar_tensor_tensor(out=ml, in0=bank[3 + i][:, :].rearrange("p (h t) -> p h t", h=2), scalar=subg,
                                               in1=mh.bitcast(F32), op0=ALU.mult, op1=ALU.subtract).then_inc(o_lo, 1)
                    else:
                        for b in range(4):
                            c0 = SEQ + 16 * (4 * (i - 2) + b)
                            last = V.scalar_tensor_tensor(
                                out=mixTl[:, ds(g * 4 + 4, 4), c0:c0 + 16],
                                in0=bank[3 + i][:, b * P:(b + 1) * P].rearrange("p (h t) -> p h t", h=4)[:, :, 0:16], scalar=subg,
                                in1=mixTh[:, ds(g * 4 + 4, 4), c0:c0 + 16].bitcast(F32), op0=ALU.mult, op1=ALU.subtract)
                        last.then_inc(o_lo, 1)

            for kq in range(AHEAD, 4):
                split_lo(BASE_POOL + kq, kq % 2)
            split_lo(BASE_WOUT, 0)
            split_lo(BASE_WOUT + 1, 1)
            dve.wait_ge(split_used, BASE_POOL + 3 + 3)
            V.memset(ub[:, :, :], 0.0).then_inc(pl_zero, 1)
            dve.wait_ge(pl_up, 5)
            src, w = ub, 1
            dsts = [sA, sB, sA, sB]
            for g in range(4):
                lo_c = 2 * w - 1
                V.tensor_tensor(dsts[g][:, g:4, lo_c:UP], src[:, g:4, lo_c:UP], src[:, g:4, lo_c - w:UP - w], ALU.add)
                drain()
                src, w = dsts[g], 2 * w
                if g == 1:
                    split_lo(BASE_WOUT + 2, 0)
            inv = cst[:, C_INV:C_INV + 64].rearrange("p (g t) -> p g t", g=4)
            for g in range(4):
                wn = 1.0 / 2 ** (g + 1)
                V.scalar_tensor_tensor(out=dT[:, g, 16:SEQ], in0=dsts[g][:, g, 32:272], scalar=wn, in1=ub[:, g, 32:272],
                                       op0=ALU.mult, op1=ALU.subtract)
                V.scalar_tensor_tensor(out=dT[:, g, SEQ:T].rearrange("p (b s) -> p b s", b=8),
                                       in0=dsts[g][:, g, 272:528].rearrange("p (b s) -> p b s", b=8)[:, :, 16:32], scalar=wn,
                                       in1=ub[:, g, 272:528].rearrange("p (b s) -> p b s", b=8)[:, :, 16:32],
                                       op0=ALU.mult, op1=ALU.subtract)
                V.tensor_tensor(dT[:, g, 0:16], dsts[g][:, g, 16:32], inv[:, g, :], ALU.mult)
                drain()
                V.tensor_tensor(dT[:, g, 0:16], dT[:, g, 0:16], ub[:, g, 16:32], ALU.subtract).then_inc(pl_d, 1)
            split_lo(BASE_WOUT + 3, 1)
            for gg in range(4):
                dve.wait_ge(pl_hi, gg + 1)
                V.scalar_tensor_tensor(out=mixTl[:, gg, :], in0=bank[3 + gg][:, 0:T], scalar=pscale[:, gg:gg + 1],
                                       in1=mixTh[:, gg, :].bitcast(F32), op0=ALU.mult, op1=ALU.subtract).then_inc(pl_lo, 1)

            def add_residual(nb, tiles=range(NT)):
                for t in tiles:
                    wait_block(dve, t, 10 + nb, BASE_WOUT + 4 * nb + 3)
                    hs = hh[:, t, nb * W:(nb + 1) * W]
                    V.tensor_tensor(hs, bank[t][:, :], hs, ALU.add).then_inc(h_done, 1)

            dve.wait_ge(h_in, 48)
            for s in range(4, 16):
                split_lo(BASE_WOUT + s, s % 2)
                if s % 4 == 0:
                    add_residual(s // 4 - 1)
            norm_part(1, hh, (g_in2, 16), lambda t: add_residual(3, (t,)))
            for s in range(16):
                split_lo(BASE_WPQ + s, s % 2)
            dve.drain().then_inc(u_turn, 2)

            def turn(m, k):
                dve.wait_ge(raw_ready[k], m * 32 + (64 * (BASE_U // 2 + 1) - 32 * k))
                dve.wait_ge(lo_done, m + (BASE_U + 1))
                V.transpose(uT[:, k, :], raw[:, k, :]).then_inc(u_turn, 1)

            def u_lo(m, k):
                dve.wait_ge(hi_done, m + (BASE_U + 1))
                V.tensor_tensor(ringL[:, k, :].rearrange("p (b r i) -> p r b i", b=KC, r=4),
                                uT[:, k, :].rearrange("p (r b i) -> p r b i", r=4, b=KC),
                                ringH[:, k, :].bitcast(F32).rearrange("p (b r i) -> p r b i", b=KC, r=4), ALU.subtract).then_inc(lo_done, 1)

            tvh = tv[:, :, :].rearrange("p (h c) k -> p h c k", c=2)
            tfh = tf[:, :, :].rearrange("p (h c) k -> p h c k", c=2)
            full = [P, PH, TOPK, TOPK]

            def route_index(t, c, part):
                if part == 0:
                    V.tensor_tensor(eqb[:, :, :, :], bhf[:, c].unsqueeze(3).broadcast_to(full),
                                    cst[:, C_IOTA:C_IOTA + 16].unsqueeze(1).unsqueeze(1).broadcast_to(full), ALU.is_equal)
                elif part == 1:
                    V.tensor_tensor(eqb[:, :, :, :], eqb[:, :, :, :], tfh[:, :, c:c + 1, :].broadcast_to(full), ALU.mult)
                else:
                    V.tensor_reduce(route[:, ds(t, 1), 1 + c, :].rearrange("p o (h k) -> p (o h) k", h=PH), eqb[:, :, :, :], AX.X, ALU.add)

            def routing_part(t, j):
                if j == 0:
                    dve.wait_ge(cur_ready, t + 1)
                    dve.sem_inc(dve_passed, 1)
                if j in (0, 3):
                    k = slice(0, 8) if j == 0 else slice(8, 16)
                    for i in range(16):
                        V.max(tv[:, i, k], sc[:, i, :])
                elif j in (1, 4):
                    k = slice(0, 8) if j == 1 else slice(8, 16)
                    for i in range(16):
                        V.max_index(ti[:, i, k], tv[:, i, k], sc[:, i, :])
                elif j == 2:
                    for i in range(16):
                        V.match_replace(sc[:, i, :], tv[:, i, 0:8], sc[:, i, :], NEG)
                elif j == 5:
                    V.tensor_copy(tf[:, :, :], ti[:, :, :]).then_inc(cur_free, 1)
                    V.tensor_tensor(cand[:, :, :].rearrange("p h (a b) -> p h a b", a=TOPK), tvh[:, :, 0, :].unsqueeze(3).broadcast_to(full),
                                    tvh[:, :, 1:2, :].broadcast_to(full), ALU.add)
                elif j in (6, 9):
                    k = slice(0, 8) if j == 6 else slice(8, 16)
                    for h in range(PH):
                        V.max(bv[:, h, k], cand[:, h, :])
                elif j in (7, 10):
                    k = slice(0, 8) if j == 7 else slice(8, 16)
                    for h in range(PH):
                        V.max_index(bi[:, h, k], bv[:, h, k], cand[:, h, :])
                elif j == 8:
                    for h in range(PH):
                        V.match_replace(cand[:, h, :], bv[:, h, 0:8], cand[:, h, :], NEG)
                elif j == 11:
                    V.tensor_copy(bst[:, 0, :], bv[:, :, 0])
                    V.tensor_scalar(bhl[:, 0], bi[:, :, :], 4, None, ALU.logical_shift_right)
                    V.tensor_scalar(bhl[:, 1], bi[:, :, :], 15, None, ALU.bitwise_and)
                    drain()
                    V.tensor_tensor(bv[:, :, :], bv[:, :, :], bst[:, 0, :].unsqueeze(2).broadcast_to([P, PH, TOPK]), ALU.subtract).then_inc(best_rdy, 1)
                    V.tensor_copy(bhf[:, :, :, :], bhl[:, :, :, :])
                elif j < 17:
                    route_index(t, (j - 12) // 3, (j - 12) % 3)
                else:
                    route_index(t, 1, 2)
                    dve.wait_ge(best_exp, t + 1)
                    V.tensor_reduce(bst[:, 0, :], bv[:, :, :], AX.X, ALU.add)
                    drain()
                    V.reciprocal(bst[:, 1, :], bst[:, 0, :])
                    drain()
                    V.tensor_tensor(route[:, ds(t, 1), 0, :].rearrange("p o (h k) -> p (o h) k", h=PH), bv[:, :, :],
                                    bst[:, 1, :].unsqueeze(2).broadcast_to([P, PH, TOPK]), ALU.mult).then_inc(rt_ready, 1)
                drain()

            def one_hots(it, qd):
                dve.wait_ge(g_mm, it * 8 + (qd + 1))
                for i in range(4):
                    tk = it * 32 + (qd * 4 + i)
                    V.tensor_scalar(onesA[:, qd % 2, i, :], iota, rT[:, 1, ds(tk, 1)], rT[:, 0, ds(tk, 1)], ALU.is_equal, ALU.mult)
                    last = V.tensor_scalar(onesB[:, qd % 2, i, :], iota, rT[:, 2, ds(tk, 1)], None, ALU.is_equal)
                last.then_inc(ab_ready, 1)

            dve.wait_ge(sc_rdy, 12)
            turn(0, 0)
            with dve.Fori(0, NT) as t:
                for j in range(N_PARTS):
                    m = t * N_PARTS + j
                    turn(m + 1, (j + 1) % 2)
                    u_lo(m, j % 2)
                    routing_part(t, j)
            dve.wait_ge(rt_ev, 2)
            with dve.Fori(0, NTB // 2) as it:
                for s in range(4):
                    m = it * 4 + (U_ROUTE + s)
                    turn(m + 1, (s + 1) % 2)
                    u_lo(m, s % 2)
                    one_hots(it, 2 * s)
                    one_hots(it, 2 * s + 1)
            with dve.Fori(0, U_REST // 2 - 1) as mp:
                for k in range(2):
                    m = mp * 2 + (U_ROUTE + U_DENSE + k)
                    turn(m + 1, (k + 1) % 2)
                    u_lo(m, k)
            turn(P - 1, 1)
            u_lo(P - 2, 0)
            u_lo(P - 1, 1)

            for k in range(2):
                dve.wait_ge(a_store[k], 16 * 64)
                dve.wait_ge(g_store[k], 16 * 12)
            V.memset(zero[:, :], 0.0).then_inc(z_done, 1)
            dve.sem_inc(w_mult, 8)
            for dh in range(2):
                with dve.Fori(0, 8) as it:
                    for s in range(8):
                        slot = s % 2
                        dve.wait_ge(a_in[slot], it * 64 + 16 * (dh * 32 + s // 2 + 1))
                        dve.wait_ge(gg_in[s // 4], it * 16 + 16 * (dh * 8 + 1))
                        V.tensor_tensor(wt[:, slot, :, :].rearrange("p q (b t) -> p q b t", t=TB),
                                        at_[:, slot, :, :].rearrange("p q (b t) -> p q b t", t=TB),
                                        gt[:, s // 4, :, :].rearrange("p b (q t) -> p q b t", q=8)[:, 2 * (s % 4):2 * (s % 4) + 2, :, :],
                                        ALU.mult).then_inc(w_mult, 1)
                        split_lo(it * 8 + (BASE_V + dh * 64 + s), slot)
                        dve.wait_ge(wh_done, it * 8 + (dh * 64 + s + 1))
                        V.tensor_tensor(xTl[:, 2 * slot:2 * slot + 2, :], wt[:, slot, :, :],
                                        xTh[:, 2 * slot:2 * slot + 2, :].bitcast(F32), ALU.subtract).then_inc(wl_done, 1)
                dve.wait_ge(acc_done, dh + 1)
                for t in range(NT):
                    for c in range(2):
                        ysl = hh[:, t, dh * 1024 + c * W:dh * 1024 + (c + 1) * W]
                        V.tensor_tensor(ysl, bank[2 * t + c][:, :], ysl, ALU.add).then_inc(y_done, 1)

        @block.tensor
        def _(pe):
            MM, TR = nc.tensor.matmul, nc.tensor.transpose
            for one in (p_WT, s_S, s_w):
                pe.sem_inc(one, 1)
            pe.sem_inc(split_used, 2)
            pe.sem_inc(s_o, 2)
            pe.sem_inc(s_kt, 2)
            pe.sem_inc(g_mm, 2)
            pe.wait_ge(S_const, 16)

            def norm_part(p):
                for t in range(NT):
                    pe.wait_ge(xs_ready, p * 3 + t + 1)
                    for q in range(4):
                        n = p * 12 + t * 4 + q
                        if n >= 4:
                            pe.wait_ge(tr_free, n - 3)
                        for i in range(4):
                            k = 4 * q + i
                            last = TR(bank[3 + q][:, i * P:(i + 1) * P], xs[:, t % 2, k * P:(k + 1) * P], ident)
                        last.then_inc(tr_ready, 1)
                pe.wait_ge(tr_free, p * 12 + 12)

            def three(out, h1, l1, h2, l2, first, last):
                MM(out, h1, h2, start=first, stop=False)
                MM(out, h1, l2, start=False, stop=False)
                return MM(out, l1, h2, start=False, stop=last)

            def weight_tile(n, slot, kq, t, xh, xl, free, order=(0, 1, 2, 3)):
                if t == 0:
                    pe.wait_ge(lo_done, n + 3)
                begin, end = kq == order[0], kq == order[3]
                if begin:
                    pe.wait_ge(*free(t))
                for k in range(KQ):
                    c = slice(k * W, (k + 1) * W)
                    ts = slice(t * P, (t + 1) * P)
                    last = three(bank[t][:, :], xh[:, kq * KQ + k, ts], xl[:, kq * KQ + k, ts],
                                 ringH[:, slot, c], ringL[:, slot, c], begin and k == 0, end and k == KQ - 1)
                if t == NT - 1:
                    last.then_inc(split_used, 1)
                elif end:
                    last.then_inc(proj_ready, 1)

            def weight_step(n, slot, kq, xh, xl, free):
                for t in range(NT):
                    weight_tile(n, slot, kq, t, xh, xl, free)

            norm_part(0)
            pe.sem_inc(proj_free, 3)
            for s in range(AHEAD):
                weight_step(s, s % 2, s, xTh, xTl, lambda t: (proj_free, t + 1))
            with pe.Fori(0, NG) as g:
                def w_in_tile(s, t):
                    weight_tile(g * 12 + s, s % 2, s % 4, t, xTh, xTl, lambda t: (proj_free, g * 9 + (s // 4 * 3 + t + 1)))

                for s in range(AHEAD, 12):
                    for t in range(NT - 1 if s == 11 else NT):
                        w_in_tile(s, t)

                def p_trans(h):
                    for m in range(2):
                        for t in range(2):
                            last = TR(bank[0][:, (2 * m + t) * P:(2 * m + t + 1) * P], qk[:, m, t, h * P:(h + 1) * P], ident)
                    last.then_inc(p_tr, 1)

                def p_scores(h):
                    pe.wait_ge(p_qkT, g * 4 + (h + 1))
                    if h:
                        pe.wait_ge(p_exp, g * 8 + 2 * h)
                    for qt in range(2):
                        nk = P * (qt + 1)
                        for c in range(2):
                            r = slice(64 * c, 64 * c + 64)
                            last = MM(pS[qt][:, c, :], qkT[r, h % 2, qt * P:(qt + 1) * P],
                                      qkT[r, h % 2, 256:256 + nk], start=True, stop=True)
                    last.then_inc(p_S, 1)

                def p_turn(m):
                    pe.wait_ge(p_W, g * 8 + (m + 1))
                    pe.wait_ge(p_oe, g * 8 + (m + 1))
                    for kt in range(m % 2 + 1):
                        last = TR(bank[3][:, kt * P:(kt + 1) * P], Wp[:, kt * P:(kt + 1) * P], ident)
                    last.then_inc(p_WT, 1)

                def p_values(m):
                    h, qt = divmod(m, 2)
                    pe.wait_ge(p_WTe, g * 8 + (m + 1))
                    for kt in range(qt + 1):
                        last = MM(bank[3][:, 0:P], WTp[:, kt, :], vs[:, kt, h * P:(h + 1) * P], start=kt == 0, stop=kt == qt)
                    last.then_inc(p_o, 1)

                def s_trans(b):
                    pe.wait_ge(kc_in[b % 2], g * 64 + 16 * (b // 2 + 1))
                    pe.wait_ge(s_kTe, g * 8 + (b + 1))
                    for h in range(HG):
                        for c in range(2):
                            last = TR(bank[4 + h // 2][:, (h % 2) * 256 + c * P:(h % 2) * 256 + (c + 1) * P],
                                      kc[:, b % 2, c, h * P:(h + 1) * P], ident)
                    last.then_inc(s_kt, 1)

                def s_scores(b):
                    pe.wait_ge(s_kTe, g * 8 + (b + 2))
                    pe.wait_ge(s_q, g * 8 + (b + 1))
                    pe.wait_ge(s_exp, g * 8 + (b + 1))
                    for h in range(HG):
                        r = slice(32 * h, 32 * h + 32)
                        MM(bank[6][r, 0:256], qcur[:, h, :], kTc[:, b % 2, h, :], start=True, stop=True)
                        last = MM(bank[6][r, 256:384], qcur[:, h, :], kTn[:, h, :], start=True, stop=True)
                    last.then_inc(s_S, 1)

                pe.wait_ge(o_lo, g * 4 + 1)
                s_trans(0)
                pe.wait_ge(qk_ready, g * 2 + 2)
                for m, bk in ((0, 6), (1, 7)):
                    for h in range(HG):
                        last = TR(bank[bk][:, h * P:(h + 1) * P], qk[:, m, 2, h * P:(h + 1) * P], ident)
                    last.then_inc(sT, 1)
                w_in_tile(11, 2)
                pe.wait_ge(proj_free, g * 9 + (3 + 7))
                p_trans(0)
                pe.wait_ge(sTe, g * 2 + 2)
                s_scores(0)
                pe.wait_ge(proj_free, g * 9 + (3 + 9))
                p_scores(0)
                for b in range(DEC_B):
                    if b + 1 < DEC_B:
                        s_trans(b + 1)
                    p_turn(b)
                    if b % 2 == 0 and b + 2 < DEC_B:
                        p_trans(b // 2 + 1)
                    if b % 2 == 1 and b + 1 < DEC_B:
                        p_scores(b // 2 + 1)
                    if b == 6:
                        w_in_tile(12, 0)
                    if b == 7:
                        w_in_tile(12, 2)
                    pe.wait_ge(s_M, g * 8 + (b + 1))
                    pe.wait_ge(s_oe, g * 8 + (b + 1))
                    for c in range(3):
                        last = MM(bank[7][:, c * P:(c + 1) * P], Ps[:, c * P:(c + 1) * P], Ms[:, :], start=True, stop=True)
                    last.then_inc(s_w, 1)
                    p_values(b)
                    if b + 1 < DEC_B:
                        s_scores(b + 1)
                    if b == 6:
                        pe.wait_ge(p_exp, g * 8 + 8)
                        w_in_tile(12, 1)
                    if b == 7:
                        w_in_tile(13, 0)
                    pe.wait_ge(s_we, g * 8 + (b + 2))
                    pe.wait_ge(vc_in[b % 2], g * 64 + 16 * (b // 2 + 1))
                    for h in range(HG):
                        for c in range(3):
                            rhs = vc[:, b % 2, c, h * P:(h + 1) * P] if c < 2 else vs[:, 2, h * P:(h + 1) * P]
                            last = MM(bank[7][32 * h:32 * h + 32, 0:P], wTs[:, c, 32 * h:32 * h + 32], rhs, start=c == 0, stop=c == 2)
                    last.then_inc(s_o, 1)
                w_in_tile(13, 1)
                w_in_tile(13, 2)
                for t in range(NT):
                    w_in_tile(14, t)
                pe.wait_ge(o_n, g + 1)
                for i in range(4):
                    for j in range(4):
                        last = TR(bank[3 + i][:, j * P:(j + 1) * P], oall[:, 4 * i + j, :], ident)
                    last.then_inc(o_t, 1)

            for kq in range(AHEAD, 4):
                weight_step(BASE_POOL + kq, kq % 2, kq, xTh, xTl, lambda t: (proj_free, 27 + t + 1))
            def w_out_tile(i, t):
                nb, pos = divmod(i, 4)
                weight_tile(BASE_WOUT + i, i % 2, W_OUT_ORDER[pos], t, mixTh, mixTl,
                            lambda t: (h_done, (nb - 1) * 3 + t + 1) if nb else (proj_free, 30 + t + 1), W_OUT_ORDER)

            pe.wait_ge(o_lo, 13)
            for t in range(NT):
                w_out_tile(0, t)
            for gg in range(4):
                for t in range(NT):
                    last = TR(bank[3 + gg][:, t * P:(t + 1) * P], ptok[:, t, gg * P:(gg + 1) * P], ident)
                last.then_inc(pl_tr, 1)
            pe.wait_ge(pl_in, 32)
            nh = DEC_B * HIST
            for gg in range(4):
                last = TR(bank[7][:, gg * nh:(gg + 1) * nh], hist[0:nh, gg * P:(gg + 1) * P], cst[0:nh, C_ID:C_ID + nh])
            last.then_inc(pl_tr, 1)
            for t in range(NT):
                w_out_tile(1, t)
            w_out_tile(2, 0)
            w_out_tile(2, 1)
            for gg in range(4):
                pe.wait_ge(pl_d, gg + 1)
                MM(bank[3 + gg][:, 0:T], wpl[:, gg, :], dT[:, gg, :], start=True, stop=True).then_inc(pl_mm, 1)
            w_out_tile(2, 2)
            pe.wait_ge(pl_lo, 4)
            for i in range(3, 16):
                for t in range(NT):
                    w_out_tile(i, t)
            norm_part(1)

            pe.wait_ge(key_in, 16)
            for c in range(2):
                last = TR(bank[7][:, c * P:(c + 1) * P], keyr[:, c, :], ident)
            last.then_inc(key_tr, 1)
            pe.wait_ge(key_ev, 1)

            def key_scores(nb):
                pe.wait_ge(qT_ev, nb * 4 + 4)
                if nb:
                    pe.wait_ge(sc_ev, nb * 3)
                for t in range(NT):
                    for sub in range(4):
                        last = MM(bank[4 + t][:, sub * P:(sub + 1) * P], qTk[:, sub, t * P:(t + 1) * P], keyT[:, sub % 2, :],
                                  start=True, stop=True)
                    last.then_inc(sc_rdy, 1)

            pe.wait_ge(h_done, 12)
            for nb in range(4):
                for kq in range(4):
                    n = BASE_WPQ + nb * 4 + kq
                    pe.wait_ge(lo_done, n + 3)
                    for sub in range(4):
                        if kq == 0 and nb:
                            pe.wait_ge(qT_ev, (nb - 1) * 4 + sub + 1)
                        for k in range(KQ):
                            c = slice(k * W + sub * P, k * W + (sub + 1) * P)
                            last = three(bank[sub][:, 0:T], ringH[:, kq % 2, c], ringL[:, kq % 2, c],
                                         xTh[:, kq * KQ + k, :], xTl[:, kq * KQ + k, :], kq == 0 and k == 0, kq == 3 and k == KQ - 1)
                        if sub == 3:
                            last.then_inc(split_used, 1)
                        elif kq == 3:
                            last.then_inc(qT_rdy, 1)
                    if kq == 0 and nb:
                        key_scores(nb - 1)
            key_scores(3)

            def u_step(m, k):
                pe.wait_ge(lo_done, m + (BASE_U + 3))
                pe.wait_ge(gelu_done, m + 1)
                for b in range(KC):
                    c = slice(b * P, (b + 1) * P)
                    last = three(bank[k][:, 0:T], ringH[:, k, c], ringL[:, k, c], xTh[:, b, :], xTl[:, b, :], b == 0, b == KC - 1)
                last.then_inc(split_used, 1)

            def dense_weights(it, qd):
                pe.wait_ge(ab_ready, it * 8 + (qd + 1))
                pe.wait_ge(g_ev, it * 8 + (qd + 1))
                for i in range(4):
                    last = MM(bank[6 + qd % 2][:, i * P:(i + 1) * P], onesA[:, qd % 2, i, :], onesB[:, qd % 2, i, :],
                              start=True, stop=True)
                last.then_inc(g_mm, 1)

            with pe.Fori(0, U_ROUTE // 2) as mp:
                for k in range(2):
                    u_step(mp * 2 + k, k)
            pe.wait_ge(rt_ready, 3)
            pe.wait_ge(sc_ev, 12)
            for i in range(3):
                for t in range(NT):
                    last = TR(bank[4 + i][:, t * P:(t + 1) * P], route[:, t, i, :], ident)
                last.then_inc(rt_tr, 1)
            pe.wait_ge(rt_ev, 2)
            with pe.Fori(0, NTB // 2) as it:
                for s in range(4):
                    u_step(it * 4 + (U_ROUTE + s), s % 2)
                    for qd in range(2 * s, 2 * s + 2):
                        dense_weights(it, qd)
            with pe.Fori(0, U_REST // 2) as mp:
                for k in range(2):
                    u_step(mp * 2 + (U_ROUTE + U_DENSE + k), k)

            pe.wait_ge(z_done, 2)
            pe.wait_ge(gelu_done, P + 2)
            for dh in range(2):
                if dh:
                    pe.wait_ge(y_done, 6)
                for i in range(6):
                    MM(bank[i][:, :], zero[:, 0:P], zero[:, :], start=True, stop=False)
                with pe.Fori(0, 8) as it:
                    for s in range(8):
                        slot = s % 2
                        pe.wait_ge(lo_done, it * 8 + (BASE_V + dh * 64 + s + 3))
                        pe.wait_ge(wl_done, it * 8 + (dh * 64 + s + 1))
                        for q in range(2):
                            for t in range(NT):
                                for c in range(2):
                                    cs = slice(q * 1024 + c * W, q * 1024 + (c + 1) * W)
                                    last = three(bank[2 * t + c][:, :], xTh[:, 2 * slot + q, t * P:(t + 1) * P],
                                                 xTl[:, 2 * slot + q, t * P:(t + 1) * P], ringH[:, slot, cs], ringL[:, slot, cs],
                                                 False, False)
                        last.then_inc(split_used, 1)
                for i in range(6):
                    last = MM(bank[i][:, :], zero[:, 0:P], zero[:, :], start=False, stop=True)
                last.then_inc(acc_done, 1)


INS = ["x_prompt", "x_sample", "cache_k", "cache_v", "state_pool", "norm1_g", "w_in", "w_pool", "pool_scale", "q_norm_g",
       "k_norm_g", "lambda_q1", "lambda_k1", "lambda_q2", "lambda_k2", "subln_g", "w_out", "norm2_g", "w_pq", "sub_keys",
       "u_tab", "v_tab"]
OUTS = [("y_prompt", (1, SEQ, D)), ("y_sample", (DEC_B, DEC_S, D)), ("k_prompt", (1, 1, SEQ, HEADS, 2, HD)),
        ("v_prompt", (1, 1, SEQ, HEADS, VD)), ("pool_prompt", (1, 1, HIST, DPOOL)),
        ("k_sample", (1, DEC_B, DEC_S, HEADS, 2, HD)), ("v_sample", (1, DEC_B, DEC_S, HEADS, VD)),
        ("pool_sample", (1, DEC_B, HIST, DPOOL))]


def kernel(**inputs):
    import numpy as _np
    import concourse.bacc as _bacc
    from concourse import mybir as _mybir
    from concourse.bass_utils import run_bass_kernel_spmd as _run

    nc = _bacc.Bacc("TRN2", target_bir_lowering=False, num_devices=1)
    arrays, ins, outs = {"in_cst": constants()}, {}, {}
    for name in INS:
        arrays["in_" + name] = _np.ascontiguousarray(inputs[name])
    for name, a in arrays.items():
        ins[name[3:]] = nc.dram_tensor(name, a.shape, _mybir.dt.from_np(a.dtype), kind="ExternalInput").ap()
    for name, shape in OUTS:
        outs[name] = nc.dram_tensor("out_" + name, shape, _mybir.dt.float32, kind="ExternalOutput").ap()
    hybrid_layer(nc, ins, outs)
    r = _run(nc, [arrays], core_ids=[0])
    return tuple(r.results[0]["out_" + name] for name, _ in OUTS)
```
